# Optimizing a Trainium2 kernel written in Bass

```python
import jax, jax.numpy as jnp
from jax import lax
import numpy as np

D_MODEL = 2048
BATCH = 1
SEQ = 1024
DEPTH = 1

CHUNK = 64
EPS = 1e-6
NEG_INF = -1e30

A_HEADS = 6
A_DK = 128
A_DV = 128
A_QF = A_HEADS * A_DK
A_WIDTH = A_HEADS * A_DV

B_HEADS = 5
B_DH = 128
B_WIDTH = B_HEADS * B_DH
B_PREV_CHUNKS = 8
B_BAND = B_PREV_CHUNKS + 1
REL_CLIP = 128

C_HEADS = 5
C_DK = 64
C_DV = 128
C_QK = C_HEADS * C_DK
C_WIDTH = C_HEADS * C_DV
ROPE_BASE = 10000.0

D_MIX = A_WIDTH + B_WIDTH + C_WIDTH
SPLIT_SIZES = (A_QF, A_QF, A_WIDTH, A_WIDTH,
               B_WIDTH, B_WIDTH, B_WIDTH, B_WIDTH,
               C_QK, C_QK, C_WIDTH, C_WIDTH)
D_IN = 2 * A_QF + 2 * A_WIDTH + 4 * B_WIDTH + 2 * C_QK + 2 * C_WIDTH

kernel_name = "hybrid_hgrn2_bandattn_retention"

def rmsnorm(x, gain):
    x32 = x.astype(jnp.float32)
    y = x32 * lax.rsqrt(jnp.mean(x32 * x32, axis=-1, keepdims=True) + EPS)
    return (y * gain.astype(jnp.float32)).astype(x.dtype)

def split_columns(t):
    parts, start = [], 0
    for size in SPLIT_SIZES:
        parts.append(t[..., start:start + size])
        start += size
    return parts

def hgrn2_group(q, f_logit, i, lb, gain):
    f32 = jnp.float32
    bsz, s, _ = q.shape
    n = s // CHUNK
    lb = lb.astype(f32)
    z = f_logit.astype(f32)
    log_f = jnp.logaddexp(jnp.log(lb), jnp.log1p(-lb) + jax.nn.log_sigmoid(z))
    k = (1.0 - lb) * jax.nn.sigmoid(-z)
    q = jax.nn.silu(q.astype(f32)) * (A_DK ** -0.5)

    def to_chunks(t, d):
        return t.reshape(bsz, n, CHUNK, A_HEADS, d).transpose(1, 0, 3, 2, 4)

    qc, kc, gc = to_chunks(q, A_DK), to_chunks(k, A_DK), to_chunks(log_f, A_DK)
    vc = to_chunks(i.astype(f32), A_DV)
    causal = jnp.tril(jnp.ones((CHUNK, CHUNK), dtype=bool))

    def step(state, inp):
        qn, kn, vn, gn = inp
        b = jnp.cumsum(gn, axis=2)
        b_last = b[:, :, -1:, :]
        o_inter = jnp.einsum('bhtk,bhkv->bhtv', qn * jnp.exp(b), state)
        diff = b[:, :, :, None, :] - b[:, :, None, :, :]
        decay = jnp.exp(jnp.where(causal[:, :, None], diff, -jnp.inf))
        scores = jnp.einsum('bhtsk,bhsk->bhts', qn[:, :, :, None, :] * decay, kn)
        o = o_inter + jnp.einsum('bhts,bhsv->bhtv', scores, vn)
        new_state = (jnp.exp(b_last[:, :, 0, :])[..., None] * state
                     + jnp.einsum('bhsk,bhsv->bhkv', kn * jnp.exp(b_last - b), vn))
        return new_state, o

    s0 = jnp.zeros((bsz, A_HEADS, A_DK, A_DV), f32)
    _, o = lax.scan(step, s0, (qc, kc, vc, gc))
    o = o * lax.rsqrt(jnp.mean(o * o, axis=-1, keepdims=True) + EPS) * gain.astype(f32)
    return o.transpose(1, 0, 3, 2, 4).reshape(bsz, s, A_WIDTH)

def band_attention_group(q, k, v, rel_bias):
    f32 = jnp.float32
    bsz, s, _ = q.shape
    n = s // CHUNK

    def to_chunks(t):
        return t.reshape(bsz, n, CHUNK, B_HEADS, B_DH).transpose(0, 3, 1, 2, 4)

    qc, kc, vc = to_chunks(q), to_chunks(k), to_chunks(v)
    pad = ((0, 0), (0, 0), (B_PREV_CHUNKS, 0), (0, 0), (0, 0))
    band_idx = jnp.arange(n)[:, None] + jnp.arange(B_BAND)[None, :]
    k_band = jnp.pad(kc, pad)[:, :, band_idx].reshape(bsz, B_HEADS, n, B_BAND * CHUNK, B_DH)
    v_band = jnp.pad(vc, pad)[:, :, band_idx].reshape(bsz, B_HEADS, n, B_BAND * CHUNK, B_DH)

    q_pos = jnp.arange(CHUNK)
    k_pos = jnp.arange(B_BAND * CHUNK) - B_PREV_CHUNKS * CHUNK
    rel = q_pos[:, None] - k_pos[None, :]
    bias = rel_bias[:, jnp.clip(rel, -REL_CLIP, REL_CLIP) + REL_CLIP].astype(f32)
    valid = (jnp.arange(n)[:, None] + jnp.arange(B_BAND * CHUNK)[None, :] // CHUNK) >= B_PREV_CHUNKS

    scores = jnp.einsum('bhnqd,bhnkd->bhnqk', qc, k_band, preferred_element_type=f32)
    scores = scores * (B_DH ** -0.5) + bias[None, :, None]
    scores = jnp.where(valid[None, None, :, None, :], scores, NEG_INF)
    p = jax.nn.softmax(scores, axis=-1)
    o = jnp.einsum('bhnqk,bhnkd->bhnqd', p.astype(v_band.dtype), v_band, preferred_element_type=f32)
    return o.transpose(0, 2, 3, 1, 4).reshape(bsz, s, B_WIDTH)

def apply_rotary(t, cos, sin):
    t1, t2 = t[..., :C_DK // 2], t[..., C_DK // 2:]
    c, s = cos[None, :, None, :], sin[None, :, None, :]
    return jnp.concatenate([t1 * c - t2 * s, t1 * s + t2 * c], axis=-1)

def retention_group(q, k, v, cos, sin):
    f32 = jnp.float32
    bsz, s, _ = q.shape
    n = s // CHUNK
    q = apply_rotary(q.astype(f32).reshape(bsz, s, C_HEADS, C_DK), cos, sin)
    k = apply_rotary(k.astype(f32).reshape(bsz, s, C_HEADS, C_DK), cos, sin) * (C_DK ** -0.5)

    def to_chunks(t, d):
        return t.reshape(bsz, n, CHUNK, C_HEADS, d).transpose(0, 3, 1, 2, 4)

    qc, kc = to_chunks(q, C_DK), to_chunks(k, C_DK)
    vc = to_chunks(v.astype(f32).reshape(bsz, s, C_HEADS, C_DV), C_DV)

    log_gamma = jnp.log1p(-jnp.exp2(-5.0 - jnp.arange(C_HEADS, dtype=f32)))
    pos = jnp.arange(CHUNK, dtype=f32)
    rel = pos[:, None] - pos[None, :]
    decay_mask = jnp.where(rel >= 0, jnp.exp(log_gamma[:, None, None] * jnp.maximum(rel, 0.0)), 0.0)

    scores = jnp.einsum('bhnik,bhnjk->bhnij', qc, kc) * decay_mask[None, :, None]
    o_intra = jnp.einsum('bhnij,bhnjv->bhniv', scores, vc)

    k_dec = kc * jnp.exp(log_gamma[:, None] * (CHUNK - 1 - pos)[None, :])[None, :, None, :, None]
    d_state = jnp.einsum('bhnjk,bhnjv->bhnkv', k_dec, vc)
    chunk_decay = jnp.exp(log_gamma * CHUNK)[None, :, None, None]

    def step(state, ds):
        return chunk_decay * state + ds, state

    s0 = jnp.zeros((bsz, C_HEADS, C_DK, C_DV), f32)
    _, prev_state = lax.scan(step, s0, d_state.transpose(2, 0, 1, 3, 4))
    prev_state = prev_state.transpose(1, 2, 0, 3, 4)
    q_dec = qc * jnp.exp(log_gamma[:, None] * (pos + 1.0)[None, :])[None, :, None, :, None]
    o = o_intra + jnp.einsum('bhnik,bhnkv->bhniv', q_dec, prev_state)
    o = o * lax.rsqrt(jnp.mean(o * o, axis=-1, keepdims=True) + EPS)
    return o.transpose(0, 2, 3, 1, 4).reshape(bsz, s, C_WIDTH)

def hybrid_layer(x, w_in, norm_gain, lb, hgrn_gain, rel_bias, w_out, cos, sin):
    h = rmsnorm(x, norm_gain)
    proj = jnp.einsum('bsd,de->bse', h, w_in)
    aq, af, ai, ag, bq, bk, bv, bg, cq, ck, cv, cg = split_columns(proj)
    ya = hgrn2_group(aq, af, ai, lb, hgrn_gain).astype(x.dtype) * jax.nn.silu(ag)
    yb = band_attention_group(bq, bk, bv, rel_bias).astype(x.dtype) * jax.nn.silu(bg)
    yc = retention_group(cq, ck, cv, cos, sin).astype(x.dtype) * jax.nn.silu(cg)
    y = jnp.concatenate([ya, yb, yc], axis=-1)
    return x + jnp.einsum('bse,ed->bsd', y, w_out)

def setup_inputs(seed: int = 0) -> dict:
    key = jax.random.key(seed)
    ks = jax.random.split(key, 8)
    x = jax.random.normal(ks[0], (BATCH, SEQ, D_MODEL), jnp.float32)
    w_in = jax.random.normal(ks[1], (DEPTH, D_MODEL, D_IN), jnp.float32) * D_MODEL ** -0.5
    norm_gain = 1.0 + 0.05 * jax.random.normal(ks[2], (DEPTH, D_MODEL), jnp.float32)
    lb_logits = 0.5 * jax.random.normal(ks[3], (DEPTH, A_QF), jnp.float32)
    hgrn_norm_gain = 1.0 + 0.05 * jax.random.normal(ks[4], (DEPTH, A_DV), jnp.float32)
    rel_bias = 0.1 * jax.random.normal(ks[5], (DEPTH, B_HEADS, 2 * REL_CLIP + 1), jnp.float32)
    w_out = jax.random.normal(ks[6], (DEPTH, D_MIX, D_MODEL), jnp.float32) * D_MIX ** -0.5
    final_gain = 1.0 + 0.05 * jax.random.normal(ks[7], (D_MODEL,), jnp.float32)
    return {"x": x, "w_in": w_in, "norm_gain": norm_gain, "lb_logits": lb_logits,
            "hgrn_norm_gain": hgrn_norm_gain, "rel_bias": rel_bias, "w_out": w_out,
            "final_gain": final_gain}

def reference(x, w_in, norm_gain, lb_logits, hgrn_norm_gain, rel_bias, w_out, final_gain):
    s = x.shape[1]
    lb_all = jnp.cumsum(jax.nn.softmax(lb_logits.astype(jnp.float32), axis=0), axis=0)
    lb_all = lb_all - lb_all[0:1]
    inv_freq = ROPE_BASE ** (-jnp.linspace(0.0, 1.0, C_DK // 2, dtype=jnp.float32))
    ang = jnp.arange(s, dtype=jnp.float32)[:, None] * inv_freq[None, :]
    cos, sin = jnp.cos(ang), jnp.sin(ang)
    for layer in range(DEPTH):
        x = hybrid_layer(x, w_in[layer], norm_gain[layer], lb_all[layer], hgrn_norm_gain[layer],
                         rel_bias[layer], w_out[layer], cos, sin)
    return rmsnorm(x, final_gain)


_drawn_inputs = setup_inputs


def setup_inputs(seed=0):
    import zlib

    import numpy as np

    out = dict(_drawn_inputs(seed))
    spreads = {}
    factors = {'hgrn_norm_gain': 3.414, 'rel_bias': 29.628}
    for name, (base, spread) in spreads.items():
        noise = np.random.default_rng([zlib.crc32(name.encode()), seed]).standard_normal(out[name].shape)
        drawn = base * np.exp(spread * noise) if base else spread * noise
        out[name] = __import__('jax').numpy.asarray(drawn.astype(out[name].dtype))
    for name, factor in factors.items():
        out[name] = (out[name] * factor).astype(out[name].dtype)
    return out
```

```python
from contextlib import ExitStack

import numpy as np
import concourse.bass as bass
from concourse import mybir

F32 = mybir.dt.float32
F32R = mybir.dt.float32r
I8 = mybir.dt.int8
ALU = mybir.AluOpType
ACT = mybir.ActivationFunctionType
AX_X = mybir.AxisListType.X

P = 128
D_MODEL, SEQ = 2048, 1024
KB = D_MODEL // P
GRAN = 4
NG = KB // GRAN
BLK = SEQ // P
HALF = 512
EPS = 1e-6
NEG_INF = -1e30
SAFE = 40.0

A_HEADS, A_DK = 6, 128
B_HEADS, B_DH, B_BAND = 5, 128, 5
C_HEADS, C_DK = 5, 64
REL = 2 * 128 + 1
BAND = B_BAND * P
A0, B0, C0 = 0, A_HEADS, A_HEADS + B_HEADS
UNITS = A_HEADS + B_HEADS + C_HEADS
TA, TB = 0, 4 * A_HEADS
TC = TB + 4 * B_HEADS
TO = TC + 3 * C_HEADS
TILES = TO + D_MODEL // P
LEVELS = [64, 32, 16, 8, 4, 2, 1]
NL = len(LEVELS)

A_M0, A_M1 = 6, 7
B_M0, B_M1 = 1 + BLK, 2 * BLK
C_M0, C_M1 = 4, 3
M0_B, M1_B = A_HEADS * A_M0, A_HEADS * A_M1
M0_C, M1_C = M0_B + B_HEADS * B_M0, M1_B + B_HEADS * B_M1
M0_O = M0_C + C_HEADS * C_M0


def shape_tables():
    t = np.arange(P)
    ident = np.eye(P, dtype=np.float32)
    level = np.zeros((P, NL, P), np.float32)
    for n, size in enumerate(LEVELS):
        same = (t[:, None] // (2 * size)) == (t[None, :] // (2 * size))
        level[:, n] = same & ((t[:, None] // size) % 2 == 0) & ((t[None, :] // size) % 2 == 1)
    start = np.ones((P, HALF), np.float32)
    start[:, ::P] = 0
    swap = np.zeros((P, P), np.float32)
    half = C_DK // 2
    for base in (0, C_DK):
        for j in range(half):
            swap[base + half + j, base + j] = -1.0
            swap[base + j, base + half + j] = 1.0
    freq = np.float32(10000.0) ** (-np.linspace(0.0, 1.0, half, dtype=np.float32))
    ang = np.arange(SEQ, dtype=np.float32)[:, None] * freq[None, :].astype(np.float32)
    cos = np.tile(np.cos(ang).astype(np.float32).T, (4, 1))
    sin = np.tile(np.sin(ang).astype(np.float32).T, (4, 1))
    dec = np.zeros((C_HEADS, P, 2 * P + 2), np.float32)
    for h in range(C_HEADS):
        lg = np.log1p(-np.exp2(-5.0 - h))
        rel = t[None, :] - t[:, None]
        dec[h, :, 0:P] = np.where(rel >= 0, np.exp(lg * np.maximum(rel, 0)), 0.0)
        dec[h, :, P:2 * P] = np.exp(lg * (t + 1.0))[None, :]
        dec[h, :, 2 * P] = np.exp(lg * (P - 1 - t))
        dec[h, :, 2 * P + 1] = np.exp(lg * P)
    return {"ident": ident, "level": level, "start": start, "swap": swap,
            "rot": np.stack([cos, sin]), "dec": dec}


def build(nc, xT, w, gain, lbl, hgain, relb, fgain, ident_d, level_d, start_d, swap_d, rot_d, dec_d, outT):
    y_dram = nc.dram_tensor("y_scratch", (UNITS, P, SEQ), F32, kind="Internal").ap()
    rel_dram = nc.dram_tensor("rel_scratch", (B_HEADS, BAND + P), F32, kind="Internal").ap()

    with ExitStack() as ctx:
        def sb(name, shape, dt=F32):
            return ctx.enter_context(nc.sbuf_tensor(name, shape, dt))

        def sem(name):
            return ctx.enter_context(nc.semaphore(name))

        mv_hi = sb("mv_hi", [P, KB, SEQ], F32R)
        mv_lo = sb("mv_lo", [P, KB, SEQ], F32R)
        w_raw = [sb(f"w_raw{q}", [P, GRAN, P]) for q in range(NG)]
        w_hi = [sb(f"w_hi{q}", [P, GRAN, P], F32R) for q in range(NG)]
        w_lo = [sb(f"w_lo{q}", [P, GRAN, P], F32R) for q in range(NG)]
        arena = sb("arena", [P, 16, SEQ])
        rstd = sb("rstd", [P, SEQ])
        ident = sb("ident", [P, P])
        ones = sb("ones", [P, P])
        level = sb("level", [P, NL, P], I8)
        gain_sb = sb("gain_sb", [P, KB])
        fgain_sb = sb("fgain_sb", [P, KB])
        hgain_sb = sb("hgain_sb", [P, 1])
        lb_all = sb("lb_all", [P, 4, A_HEADS])
        lb_now = sb("lb_now", [P, 4, 1])
        end_dec = sb("end_dec", [P, BLK])
        row_max = sb("row_max", [P, 2, 1])
        row_sum = sb("row_sum", [P, 2, 1])
        row_inv = sb("row_inv", [P, 2, 1])
        wait_pad = sb("wait_pad", [P, 1])
        eps_sb = sb("eps_sb", [P, 1])

        def arr(n):
            return arena[:, n, :]

        relrow = arena[0:B_HEADS, 7, 0:REL]

        level_f32 = arena[:, 8, 0:NL * P].rearrange("p (l t) -> p l t", l=NL)
        start_f32 = arena[:, 9, 0:HALF]

        def blocks(n):
            return arena[:, n, :].rearrange("p (c t) -> p c t", c=BLK)

        T1, T2, T3, GATE, VT, V, Y = range(7)
        Q, K, B, LV0, LV1, SC, ST, KDT, QE = range(7, 16)
        BQ, BK, BP0, BP1, BT0, BT1, BIAS = range(7, 14)
        CQK, CK, CQD, CSC, CST, CKT, CCOS, CSIN, CDEC = range(7, 16)
        LV = [LV0, LV1]
        bias = arena[:, BIAS, 0:BAND]
        BP, BT = [BP0, BP1], [BT0, BT1]
        swap = arena[:, CDEC, 512:512 + P]
        dec = arena[:, CDEC, 0:2 * P + 2]
        scan_mask = sb("scan_mask", [P, HALF], I8)

        prj = [ctx.enter_context(nc.psum_tensor(f"prj{n}", [P, SEQ], F32)) for n in range(2)]
        mix = [ctx.enter_context(nc.psum_tensor(f"mix{n}", [P, SEQ], F32)) for n in range(2)]

        def mixb(n):
            return mix[n][:, :].rearrange("p (c t) -> p c t", c=BLK)

        const_in = sem("const_in")
        gain_in = sem("gain_in")
        x_in = [sem(f"x_in{n}") for n in range(4)]
        w_in = [sem(f"w_in{n}") for n in range(NG)]
        w_hi_done = sem("w_hi_done")
        w_split = sem("w_split")
        w_used = sem("w_used")
        tile_evicted = sem("tile_evicted")
        filled = [sem("mix0_filled"), sem("mix1_filled")]
        drained = [sem("mix0_drained"), sem("mix1_drained")]
        h_hi = sem("h_hi")
        ones_ready = sem("ones_ready")
        h_lo = sem("h_lo")
        sq_ready = sem("sq_ready")
        sq_used = sem("sq_used")
        start_dve = sem("start_dve")
        lb_exp = sem("lb_exp")
        masks_ready = sem("masks_ready")
        rms_log = sem("rms_log")
        rstd_ready = sem("rstd_ready")
        rel_wide = sem("rel_wide")
        silu_clamped = sem("silu_clamped")
        silu_exp = sem("silu_exp")
        silu_log = sem("silu_log")
        silu_sig = sem("silu_sig")
        silu_done = sem("silu_done")
        z_ready = sem("z_ready")
        z_clamped = sem("z_clamped")
        z_exp = sem("z_exp")
        z_log = sem("z_log")
        z_sig = sem("z_sig")
        z_loglb = sem("z_loglb")
        z_under = sem("z_under")
        z_sum = sem("z_sum")
        logf_ready = sem("logf_ready")
        b_ready = sem("b_ready")
        k_ready = sem("k_ready")
        lb_copied = sem("lb_copied")
        lv_diff = sem("lv_diff")
        lv_exp = sem("lv_exp")
        lv_ready = sem("lv_ready")
        qe_exp = sem("qe_exp")
        qe_ready = sem("qe_ready")
        kd_diff = sem("kd_diff")
        kd_exp = sem("kd_exp")
        kd_ready = sem("kd_ready")
        end_ready = sem("end_ready")
        state_ready = sem("state_ready")
        osq_ready = sem("osq_ready")
        orms_ready = sem("orms_ready")
        y_ready = sem("y_ready")
        y_stored = sem("y_stored")
        bias_in = sem("bias_in")
        bias_ready = sem("bias_ready")
        p_max = sem("p_max")
        p_exp = sem("p_exp")
        p_inv = sem("p_inv")
        p_ready = sem("p_ready")
        ctab_in = sem("ctab_in")
        cdec_in = sem("cdec_in")
        c_cos = sem("c_cos")
        c_rot = sem("c_rot")
        c_k = sem("c_k")
        c_qd = sem("c_qd")
        yl_in = [sem(f"yl_in{n}") for n in range(4)]
        yl_hi = sem("yl_hi")
        yl_lo = sem("yl_lo")
        xr_in = [sem(f"xr_in{n}") for n in range(2)]
        fin_log = sem("fin_log")
        fin_rstd = sem("fin_rstd")
        out_ready = sem("out_ready")
        out_stored = sem("out_stored")

        block = ctx.enter_context(nc.Block())

        XS = [T1, T2, T3, GATE]
        SQ = [VT, V]
        YS = [12, 13, 14, 15]

        @block.sync
        def _(sp):
            def load_x(d):
                if d >= 4:
                    sp.wait_ge(h_lo, d - 3)
                    sp.wait_ge(sq_ready, d - 3)
                sp.dma_start(arr(XS[d % 4]), xT[d]).then_inc(x_in[d % 4], 16)

            def load_w(g, first=False):
                for q in range(NG):
                    if not first:
                        sp.wait_ge(w_split, g * NG + (q + 1 - NG))
                    sp.dma_start(w_raw[q][:], w[g, :, q]).then_inc(w_in[q], 16)

            sp.dma_start(gain_sb[:], gain).then_inc(gain_in, 16)
            load_x(0)
            load_x(1)
            load_w(0, first=True)
            for d in range(2, 4):
                load_x(d)
            sp.dma_start(ident[:], ident_d).then_inc(const_in, 16)
            sp.dma_start(level_f32, level_d).then_inc(const_in, 16)
            sp.dma_start(start_f32, start_d).then_inc(const_in, 16)
            sp.dma_start(fgain_sb[:], fgain).then_inc(const_in, 16)
            sp.dma_start(hgain_sb[:], hgain).then_inc(const_in, 16)
            sp.dma_start(lb_all[:, 3, :], lbl).then_inc(const_in, 16)
            sp.dma_start(relrow, relb).then_inc(const_in, 16)
            for d in range(4, KB):
                load_x(d)
            with sp.Fori(1, TILES) as g:
                load_w(g)
            for c in range(KB):
                sp.wait_ge(out_ready, c + 1)
                sp.dma_start(outT[c], arr(c)).then_inc(out_stored, 16)
            sp.wait_ge(out_stored, 16 * KB)
            sp.wait_ge(y_stored, 16 * UNITS + 16)

        @block.gpsimd
        def _(pool):
            nc.gpsimd.memset(ones[:], 1.0).then_inc(ones_ready, 1)
            nc.gpsimd.memset(eps_sb[:], EPS).then_inc(ones_ready, 1)
            pool.wait_ge(ones_ready, 1)

            def split(g, first=False):
                for q in range(NG):
                    pool.wait_ge(w_in[q], 16 * g + 16)
                    if not first:
                        pool.wait_ge(w_used, g * NG + (q + 1 - NG))
                    nc.gpsimd.tensor_tensor(w_hi[q][:], w_raw[q][:],
                                            ones[:, None, :].to_broadcast([P, GRAN, P]),
                                            ALU.mult).then_inc(w_hi_done, 1)
                    pool.wait_ge(w_hi_done, g * NG + q + 1)
                    nc.gpsimd.tensor_tensor(w_lo[q][:], w_raw[q][:], w_hi[q][:].bitcast(F32),
                                            ALU.subtract).then_inc(w_split, 1)

            split(0, first=True)
            with pool.Fori(1, TILES) as g:
                split(g)

        @block.tensor
        def _(pe):
            def nothing():
                pass

            def project(g, pair, free, stages, before=None):
                if free is not None:
                    pe.wait_ge(tile_evicted, free)
                for q in range(NG):
                    pe.wait_ge(w_split, g * NG + q + 1)
                    for kk in range(GRAN):
                        k = q * GRAN + kk
                        if before:
                            before(k)
                        for wt, mv in ((w_hi, mv_hi), (w_hi, mv_lo), (w_lo, mv_hi)):
                            for half in range(2):
                                cols = slice(half * HALF, half * HALF + HALF)
                                last = nc.tensor.matmul(
                                    prj[pair][:, cols], wt[q][:, kk, :], mv[:, k, cols],
                                    start=(k == 0 and wt is w_hi and mv is mv_hi),
                                    stop=(k == KB - 1 and wt is w_lo))
                    last.then_inc(w_used, 1)
                    stages[q]()

            def fill(n, before):
                pe.wait_ge(drained[n], before)

            def transposes(n, src, wait, value, before):
                pe.wait_ge(const_in, 112)
                pe.wait_ge(wait, value)
                fill(n, before)
                for c in range(BLK):
                    last = nc.tensor.transpose(mixb(n)[:, c, :], blocks(src)[:, c, :], ident[:])
                last.then_inc(filled[n], 1)

            def a_vtr(u):
                return transposes(0, VT, tile_evicted, 4 * u + 3, A_M0 * u + 4)

            def a_diag(u):
                def stage():
                    pe.wait_ge(silu_done, 2 * u + 1)
                    pe.wait_ge(k_ready, u + 1)
                    fill(1, A_M1 * u)
                    for c in range(BLK):
                        last = nc.tensor.matmul(mixb(1)[:, c, :], blocks(K)[:, c, :],
                                                blocks(Q)[:, c, :], start=True, stop=True)
                    last.then_inc(filled[1], 1)
                return stage

            def a_level(u, n):
                def stage():
                    m = n % 2
                    pe.wait_ge(lv_ready, 2 * (NL * u + n + 1))
                    fill(m, (A_M0 * u + n // 2) if m == 0 else (A_M1 * u + 1 + n // 2))
                    for c in range(BLK):
                        last = nc.tensor.matmul(mixb(m)[:, c, :], blocks(LV[n % 2])[:, c, :],
                                                blocks(LV[n % 2])[:, c, :], start=True, stop=True)
                    last.then_inc(filled[m], 1)
                return stage

            def a_kdtr(u):
                def stage():
                    transposes(1, T3, kd_ready, u + 1, A_M1 * u + 4)
                    a_vtr(u)
                return stage

            def a_state(u):
                def stage():
                    pe.wait_ge(drained[1], A_M1 * u + 5)
                    pe.wait_ge(drained[0], A_M0 * u + 5)
                    for c in range(BLK - 1):
                        last = nc.tensor.matmul(mixb(1)[:, c, :], blocks(KDT)[:, c, :],
                                                blocks(V)[:, c, :], start=True, stop=True)
                    last.then_inc(filled[1], 1)
                return stage

            def a_out(u):
                def stage():
                    pe.wait_ge(drained[1], A_M1 * u + 6)
                    pe.wait_ge(qe_ready, u + 1)
                    fill(0, A_M0 * u + 5)
                    for c in range(BLK):
                        last = nc.tensor.matmul(mixb(0)[:, c, :], blocks(V)[:, c, :],
                                                blocks(SC)[:, c, :], start=True, stop=(c == 0))
                        if c > 0:
                            last = nc.tensor.matmul(mixb(0)[:, c, :], blocks(ST)[:, c, :],
                                                    blocks(QE)[:, c, :], start=False, stop=True)
                    last.then_inc(filled[0], 1)
                return stage

            def sum_squares(n, value, before):
                def stage():
                    pe.wait_ge(osq_ready, value)
                    fill(n, before)
                    for half in range(2):
                        cols = slice(half * HALF, half * HALF + HALF)
                        last = nc.tensor.matmul(mix[n][:, cols], ones[:], arr(T2)[:, cols],
                                                start=True, stop=True)
                    last.then_inc(filled[n], 1)
                return stage

            def a_ss(u):
                return sum_squares(1, u + 1, A_M1 * u + 6)

            def b_scores(i, p):
                pe.wait_ge(tile_evicted, TB + 4 * i + 2)
                fill(0, M0_B + B_M0 * i + 1 + p)
                nk = min(p + 1, B_BAND)
                first = p + 1 - nk
                for lo in range(0, nk * P, HALF):
                    hi = min(nk * P, lo + HALF)
                    last = nc.tensor.matmul(mix[0][:, lo:hi], blocks(BQ)[:, p, :],
                                            arr(BK)[:, first * P + lo:first * P + hi],
                                            start=True, stop=True)
                last.then_inc(filled[0], 1)

            def b_ptr(i, p):
                pe.wait_ge(p_ready, BLK * i + p + 1)
                fill(1, M1_B + B_M1 * i + 2 * p)
                nk = min(p + 1, B_BAND)
                for j in range(nk):
                    last = nc.tensor.transpose(mixb(1)[:, j, :], blocks(BP[p % 2])[:, j, :], ident[:])
                last.then_inc(filled[1], 1)

            def b_pv(i, p):
                fill(1, M1_B + B_M1 * i + 2 * p + 1)
                nk = min(p + 1, B_BAND)
                for j in range(nk):
                    last = nc.tensor.matmul(mixb(1)[:, 5, :], blocks(V)[:, p + 1 - nk + j, :],
                                            blocks(BT[p % 2])[:, j, :], start=(j == 0),
                                            stop=(j == nk - 1))
                last.then_inc(filled[1], 1)

            def b_visit(i, n):
                def stage():
                    if n >= 2:
                        b_pv(i, n - 2)
                    if n < BLK:
                        b_scores(i, n)
                    if 1 <= n <= BLK:
                        b_ptr(i, n - 1)
                return stage

            def b_vtr(i):
                return lambda: transposes(0, VT, tile_evicted, TB + 4 * i + 3, M0_B + B_M0 * i)

            def c_swap(i):
                def stage():
                    pe.wait_ge(tile_evicted, TC + 3 * i + 1)
                    if isinstance(i, int) and i == 0:
                        pe.wait_ge(ctab_in, 48)
                    fill(0, M0_C + C_M0 * i)
                    for half in range(2):
                        cols = slice(half * HALF, half * HALF + HALF)
                        last = nc.tensor.matmul(mix[0][:, cols], swap, arr(T1)[:, cols],
                                                start=True, stop=True)
                    last.then_inc(filled[0], 1)
                return stage

            def c_ktr(i):
                return lambda: transposes(1, CQK, c_rot, i + 1, M1_C + C_M1 * i)

            def c_vtr(i):
                return lambda: transposes(0, VT, tile_evicted, TC + 3 * i + 2, M0_C + C_M0 * i + 1)

            def c_scores(i):
                def stage():
                    pe.wait_ge(c_k, i + 1)
                    pe.wait_ge(c_rot, i + 1)
                    fill(1, M1_C + C_M1 * i + 1)
                    for c in range(BLK):
                        last = nc.tensor.matmul(mixb(1)[:, c, :], blocks(CK)[0:C_DK, c, :],
                                                blocks(CQK)[0:C_DK, c, :], start=True, stop=True)
                    last.then_inc(filled[1], 1)
                return stage

            def c_state(i):
                def stage():
                    pe.wait_ge(drained[1], M1_C + C_M1 * i + 1)
                    fill(0, M0_C + C_M0 * i + 2)
                    kt = arena[:, CKT, 0:BLK * C_DK].rearrange("p (c k) -> p c k", c=BLK)
                    for c in range(BLK - 1):
                        last = nc.tensor.matmul(mixb(0)[0:C_DK, c, :], kt[:, c, :],
                                                blocks(V)[:, c, :], start=True, stop=True)
                    last.then_inc(filled[0], 1)
                return stage

            def c_out(i):
                def stage():
                    pe.wait_ge(drained[0], M0_C + C_M0 * i + 3)
                    pe.wait_ge(c_qd, i + 1)
                    fill(1, M1_C + C_M1 * i + 2)
                    for c in range(BLK):
                        last = nc.tensor.matmul(mixb(1)[:, c, :], blocks(V)[:, c, :],
                                                blocks(CSC)[:, c, :], start=True, stop=(c == 0))
                        if c > 0:
                            last = nc.tensor.matmul(mixb(1)[:, c, :], blocks(CST)[0:C_DK, c, :],
                                                    blocks(CQD)[0:C_DK, c, :], start=False, stop=True)
                    last.then_inc(filled[1], 1)
                return stage

            def c_ss(i):
                return sum_squares(0, A_HEADS + i + 1, M0_C + C_M0 * i + 3)

            def a_late(u):
                return [a_level(u, 5), a_level(u, 6), a_kdtr(u), a_state(u),
                        nothing, a_out(u), a_ss(u), nothing]

            def b_late(i):
                return [b_visit(i, 4), b_visit(i, 5), b_visit(i, 6), b_visit(i, 7),
                        b_visit(i, 8), b_visit(i, 9), nothing, nothing]

            def c_late(i):
                return [c_out(i), c_ss(i), nothing, nothing, nothing, nothing, nothing, nothing]

            none8 = [nothing] * 8

            def a_unit(u, late, start=False):
                g = 4 * u

                def need_x(k):
                    pe.wait_ge(h_lo, k + 1)
                    if k == 0:
                        pe.wait_ge(ones_ready, 1)
                    pe.wait_ge(sq_ready, k + 1)
                    for half in range(2):
                        cols = slice(half * HALF, half * HALF + HALF)
                        last = nc.tensor.matmul(mix[0][:, cols], ones[:], arr(SQ[k % 2])[:, cols],
                                                start=(k == 0), stop=(k == KB - 1))
                    last.then_inc(sq_used, 1)
                project(g, 0, None if start else g - 1, late[0:4], need_x if start else None)
                if start:
                    pe.wait_ge(const_in, 112)
                    pe.wait_ge(rms_log, 1)
                project(g + 1, 1, None if start else g, late[4:8])
                project(g + 2, 0, g + 1, [nothing, nothing, a_diag(u), a_level(u, 0)])
                project(g + 3, 1, g + 2, [a_level(u, 1), a_level(u, 2), a_level(u, 3), a_level(u, 4)])

            def b_unit(i, late):
                g = TB + 4 * i
                project(g, 0, g - 1, late[0:4])
                project(g + 1, 1, g, late[4:8])
                project(g + 2, 0, g + 1, none8[0:4])
                project(g + 3, 1, g + 2, [b_vtr_visit(i), b_visit(i, 1), b_visit(i, 2), b_visit(i, 3)])

            def b_vtr_visit(i):
                def stage():
                    b_vtr(i)()
                    b_visit(i, 0)()
                return stage

            def c_unit(i, late):
                g = TC + 3 * i
                project(g, 0, g, late[0:4])
                project(g + 1, 1, g, [nothing, c_swap(i), nothing, nothing])
                project(g + 2, 0, g + 1, [c_vtr_k(i), c_scores(i), c_state(i), nothing])

            def c_vtr_k(i):
                def stage():
                    c_ktr(i)()
                    c_vtr(i)()
                return stage

            a_unit(0, none8, start=True)
            with pe.Fori(1, A_HEADS) as u:
                a_unit(u, a_late(u - 1))
            b_unit(0, a_late(A_HEADS - 1))
            with pe.Fori(1, B_HEADS) as i:
                b_unit(i, b_late(i - 1))
            project(TC, 0, TC - 1, b_late(B_HEADS - 1)[0:4])
            b_visit(B_HEADS - 1, 8)()
            b_visit(B_HEADS - 1, 9)()
            project(TC + 1, 1, TC, [nothing, c_swap(0), nothing, nothing])
            project(TC + 2, 0, TC + 1, [c_vtr_k(0), c_scores(0), c_state(0), nothing])
            with pe.Fori(1, C_HEADS) as i:
                c_unit(i, c_late(i - 1))
            c_out(C_HEADS - 1)()
            c_ss(C_HEADS - 1)()

            def square_sum(n, first=False, last_one=False):
                pe.wait_ge(sq_ready, KB + n + 1)
                if first:
                    fill(0, M0_O)
                for half in range(2):
                    cols = slice(half * HALF, half * HALF + HALF)
                    last = nc.tensor.matmul(mix[0][:, cols], ones[:], rstd[:, cols],
                                            start=first, stop=last_one, skip_group_check=True)
                last.then_inc(sq_used, 1)

            def need_y(k):
                pe.wait_ge(yl_lo, k + 1)

            project(TO, 1, TO - 1, none8[0:4], need_y)
            project(TO + 1, 0, TO, [nothing, lambda: square_sum(0, first=True), nothing, nothing])
            with pe.Fori(1, KB // 2) as j:
                project(TO + 2 * j, 1, TO + 2 * j - 1,
                        [nothing, lambda: square_sum(2 * j - 1), nothing, nothing])
                project(TO + 2 * j + 1, 0, TO + 2 * j,
                        [nothing, lambda: square_sum(2 * j), nothing, nothing])
            square_sum(KB - 1, last_one=True)

        @block.scalar
        def _(act):
            def exp(out, src, **kw):
                return nc.scalar.activation(out, src, ACT.Exp, **kw)

            def ln(out, src, **kw):
                return nc.scalar.activation(out, src, ACT.Ln, **kw)

            def inv_rms(src, dst, count, log_done):
                act.wait_ge(ones_ready, 2)
                ln(dst, src, scale=1.0 / count, bias=eps_sb[:, 0:1]).then_inc(*log_done[0:2])
                act.wait_ge(log_done[0], log_done[2])
                return exp(dst, dst, scale=-0.5)

            def sigmoid(m):
                act.wait_ge(silu_clamped, m + 1)
                exp(arr(T2), arr(T2), scale=-1.0).then_inc(silu_exp, 1)
                act.wait_ge(silu_exp, m + 1)
                ln(arr(T2), arr(T2), bias=1.0).then_inc(silu_log, 1)
                act.wait_ge(silu_log, m + 1)
                exp(arr(T2), arr(T2), scale=-1.0).then_inc(silu_sig, 1)

            def copy_v(fills):
                act.wait_ge(filled[0], fills)
                nc.scalar.activation(arr(V), mix[0][:], ACT.Copy).then_inc(drained[0], 1)

            def store_y(u):
                act.wait_ge(y_ready, u + 1)
                act.dma_start(y_dram[u], arr(Y)).then_inc(y_stored, 16)

            nc.scalar.preload_act_table_set("natural_log_exp_and_others")
            for d in range(KB):
                act.wait_ge(x_in[d % 4], 16 * (d // 4 + 1))
                if d >= 2:
                    act.wait_ge(sq_used, d - 1)
                nc.scalar.activation(arr(SQ[d % 2]), arr(XS[d % 4]), ACT.Square).then_inc(sq_ready, 1)
            act.wait_ge(start_dve, 1)
            exp(lb_all[:, 0, :], lb_all[:, 0, :]).then_inc(lb_exp, 1)
            act.wait_ge(rel_wide, 2)
            act.dma_start(rel_dram, arena[0:B_HEADS, Y, 0:BAND + P]).then_inc(y_stored, 16)
            act.wait_ge(sq_used, KB)
            inv_rms(mix[0][:], rstd[:], D_MODEL, (rms_log, 1, 1)).then_inc(rstd_ready, 1)

            def a_unit(u):
                act.wait_ge(z_clamped, u + 1)
                exp(arr(T2), arr(T2), scale=-1.0).then_inc(z_exp, 1)
                act.wait_ge(z_exp, u + 1)
                ln(arr(T3), arr(T2), bias=1.0).then_inc(z_log, 1)
                act.wait_ge(lb_copied, u + 1)
                ln(arr(B), arr(T2), scale=lb_now[:, 0, :], bias=1.0).then_inc(z_loglb, 1)
                act.wait_ge(z_log, u + 1)
                exp(arr(K), arr(T3), scale=-1.0).then_inc(z_sig, 1)
                sigmoid(2 * u)
                act.wait_ge(b_ready, 2 * u + 2)
                exp(arr(QE), arr(B)).then_inc(qe_exp, 1)
                exp(end_dec[:, :], blocks(B)[:, :, P - 1]).then_inc(end_ready, 1)
                act.wait_ge(kd_diff, u + 1)
                exp(arr(T3), arr(T3)).then_inc(kd_exp, 1)
                for n in range(NL):
                    if n == NL - 1:
                        sigmoid(2 * u + 1)
                    act.wait_ge(lv_diff, 2 * (NL * u + n + 1))
                    exp(arr(LV[n % 2]), arr(LV[n % 2])).then_inc(lv_exp, 1)
                act.wait_ge(filled[1], A_M1 * u + 5)
                nc.scalar.activation(arr(KDT), mix[1][:], ACT.Copy).then_inc(drained[1], 1)
                copy_v(A_M0 * u + 5)
                norm(u, 2 * u + 2, 0, A_M0 * u + 6, 1, A_M1 * u + 7)
                store_y(u)

            def norm(m, gate, n_o, o_fills, n_ss, ss_fills):
                act.wait_ge(silu_done, gate)
                act.wait_ge(filled[n_o], o_fills)
                nc.scalar.activation(arr(T2), mix[n_o][:], ACT.Square).then_inc(osq_ready, 1)
                act.wait_ge(filled[n_ss], ss_fills)
                inv_rms(mix[n_ss][:], arr(T1), P, (drained[n_ss], 1, ss_fills)).then_inc(orms_ready, 1)

            with act.Fori(0, A_HEADS) as u:
                a_unit(u)

            def b_unit(i):
                act.wait_ge(drained[0], M0_B + B_M0 * i)
                act.dma_start(bias, bass.AP(tensor=rel_dram.tensor, offset=i * (BAND + P),
                                            ap=[[1, P], [1, BAND]])).then_inc(bias_in, 16)
                copy_v(M0_B + B_M0 * i + 1)
                for n in range(BLK + 2):
                    if n == 5:
                        sigmoid(2 * A_HEADS + i)
                    if n < BLK:
                        width = min(n + 1, B_BAND) * P
                        act.wait_ge(p_max, BLK * i + n + 1)
                        exp(arr(BP[n % 2])[:, 0:width], arr(BP[n % 2])[:, 0:width],
                            bias=row_max[:, n % 2, :], accum_out=row_sum[:, n % 2, :]).then_inc(p_exp, 1)
                    if 1 <= n <= BLK:
                        width = min(n, B_BAND) * P
                        act.wait_ge(filled[1], M1_B + B_M1 * i + 2 * n - 1)
                        nc.scalar.activation(arr(BT[(n - 1) % 2])[:, 0:width], mix[1][:, 0:width],
                                             ACT.Copy).then_inc(drained[1], 1)
                store_y(B0 + i)

            with act.Fori(0, B_HEADS) as i:
                b_unit(i)

            def c_unit(i):
                act.wait_ge(c_rot, i + 1)
                nc.scalar.activation(arena[0:C_DK, CK, :], arena[C_DK:P, CQK, :], ACT.Copy,
                                     scale=C_DK ** -0.5).then_inc(c_k, 1)
                copy_v(M0_C + C_M0 * i + 2)
                sigmoid(2 * A_HEADS + B_HEADS + i)
                norm(A_HEADS + i, 2 * A_HEADS + B_HEADS + i + 1, 1, M1_C + C_M1 * i + 3, 0, M0_C + C_M0 * i + 4)
                store_y(C0 + i)

            act.wait_ge(p_ready, BLK * B_HEADS)
            act.dma_start(arr(CCOS), rot_d[0]).then_inc(ctab_in, 16)
            act.dma_start(arr(CSIN), rot_d[1]).then_inc(ctab_in, 16)
            act.dma_start(swap, swap_d).then_inc(ctab_in, 16)
            with act.Fori(0, C_HEADS) as i:
                act.wait_ge(y_ready, C0 + i)
                act.dma_start(dec, dec_d[i]).then_inc(cdec_in, 16)
                c_unit(i)

            act.wait_ge(y_stored, 16 * UNITS + 16)
            for d in range(KB):
                if d >= 4:
                    act.wait_ge(yl_lo, d - 3)
                act.dma_start(arr(YS[d % 4]), y_dram[d]).then_inc(yl_in[d % 4], 16)
            for c in range(YS[0]):
                act.dma_start(arr(c), xT[c]).then_inc(xr_in[0], 16)
            act.wait_ge(yl_lo, KB)
            for c in range(YS[0], KB):
                act.dma_start(arr(c), xT[c]).then_inc(xr_in[1], 16)

            def square(c):
                act.wait_ge(tile_evicted, TO + c + 1)
                act.wait_ge(sq_used, KB + c)
                nc.scalar.activation(rstd[:], arr(c), ACT.Square).then_inc(sq_ready, 1)

            with act.Fori(0, KB) as c:
                square(c)
            act.wait_ge(sq_used, 2 * KB)
            inv_rms(mix[0][:], rstd[:], D_MODEL, (fin_log, 1, 1)).then_inc(fin_rstd, 1)

        @block.vector
        def _(dve):
            tt = nc.vector.tensor_tensor
            ts = nc.vector.tensor_scalar
            stt = nc.vector.scalar_tensor_tensor

            def evict(g, pair, dst):
                dve.wait_ge(w_used, NG * g + NG)
                return tt(arr(dst), prj[pair][:], rstd[:], ALU.mult)

            def silu_evict(g, pair, m):
                evict(g, pair, T1).then_inc(tile_evicted, 1)
                dve.wait_ge(tile_evicted, g + 1)
                ts(arr(T2), arr(T1), -SAFE, None, ALU.max).then_inc(silu_clamped, 1)

            def silu_finish(m, dst, scale):
                dve.wait_ge(silu_sig, m + 1)
                stt(out=arr(dst), in0=arr(T1), scalar=scale, in1=arr(T2), op0=ALU.mult,
                    op1=ALU.mult).then_inc(silu_done, 1)

            def states(m, n, rows, st, fills, decay):
                dve.wait_ge(filled[n], fills)
                for c in range(BLK - 1):
                    cur = blocks(st)[0:rows, c + 1, :]
                    inc = mixb(n)[0:rows, c, :]
                    if c == 0:
                        new = nc.vector.tensor_copy(cur, inc)
                    else:
                        dve.wait_ge(state_ready, (BLK - 2) * m + c)
                        new = stt(out=cur, in0=blocks(st)[0:rows, c, :], scalar=decay(c), in1=inc,
                                  op0=ALU.mult, op1=ALU.add)
                    if c < BLK - 2:
                        new.then_inc(state_ready, 1)
                    else:
                        new.then_inc(drained[n], 1)

            dve.wait_ge(gain_in, 16)
            for d in range(KB):
                dve.wait_ge(x_in[d % 4], 16 * (d // 4 + 1))
                ts(mv_hi[:, d, :], arr(XS[d % 4]), gain_sb[:, d:d + 1], None,
                   ALU.mult).then_inc(h_hi, 1)
                dve.wait_ge(h_hi, d + 1)
                stt(out=mv_lo[:, d, :], in0=arr(XS[d % 4]), scalar=gain_sb[:, d:d + 1],
                    in1=mv_hi[:, d, :].bitcast(F32), op0=ALU.mult, op1=ALU.subtract).then_inc(h_lo, 1)
            dve.wait_ge(const_in, 112)
            nc.vector.tensor_copy(level[:], level_f32).then_inc(masks_ready, 1)
            nc.vector.tensor_copy(scan_mask[:], start_f32).then_inc(masks_ready, 1)
            dve.wait_ge(masks_ready, 2)
            tt(lb_all[:, 0, :], lb_all[:, 3, :], lb_all[:, 3, :], ALU.subtract).then_inc(start_dve, 1)
            nc.vector.tensor_copy(arena[0:B_HEADS, Y, 0:REL - 2], relrow[:, 1:REL - 1]).then_inc(rel_wide, 1)
            nc.vector.tensor_copy(arena[0:B_HEADS, Y, REL - 2:BAND + P],
                                  relrow[:, REL - 1:REL].to_broadcast([B_HEADS, BAND + P - REL + 2])
                                  ).then_inc(rel_wide, 1)
            dve.wait_ge(lb_exp, 1)
            nc.vector.reciprocal(lb_all[:, 1, :], lb_all[:, 0, :]).then_inc(start_dve, 1)
            dve.wait_ge(start_dve, 2)
            tt(lb_all[:, 2, :], lb_all[:, 0, :], lb_all[:, 1, :], ALU.mult).then_inc(start_dve, 1)
            dve.wait_ge(start_dve, 3)
            tt(lb_all[:, 0, :], lb_all[:, 2, :], lb_all[:, 2, :], ALU.subtract).then_inc(start_dve, 1)
            dve.wait_ge(start_dve, 4)
            ts(lb_all[:, 1, :], lb_all[:, 0, :], -1.0, 1.0, ALU.mult, ALU.add).then_inc(start_dve, 1)
            ts(lb_all[:, 2, :], lb_all[:, 0, :], 0.0, None, ALU.is_equal).then_inc(start_dve, 1)
            dve.wait_ge(start_dve, 6)
            dve.wait_ge(y_stored, 16)
            dve.wait_ge(rstd_ready, 1)

            def lv_view(n, size):
                return arr(n).rearrange("p (a h t) -> p a h t", h=2, t=size)

            def lv_diff_of(u, n):
                size = LEVELS[n]
                if n >= 2:
                    m = n % 2
                    dve.wait_ge(filled[m], (A_M0 * u + n // 2) if m == 0 else (A_M1 * u + 1 + n // 2))
                b, lv = lv_view(B, size), lv_view(LV[n % 2], size)
                ref = b[:, :, 0, size - 1:size].to_broadcast([P, SEQ // (2 * size), size])
                tt(lv[:, :, 1, :], b[:, :, 1, :], ref, ALU.subtract).then_inc(lv_diff, 1)
                tt(lv[:, :, 0, :], ref, b[:, :, 0, :], ALU.subtract).then_inc(lv_diff, 1)

            def lv_mult(u, n):
                size = LEVELS[n]
                lv = lv_view(LV[n % 2], size)
                dve.wait_ge(lv_exp, NL * u + n + 1)
                tt(lv[:, :, 1, :], lv[:, :, 1, :], lv_view(Q, size)[:, :, 1, :], ALU.mult).then_inc(lv_ready, 1)
                tt(lv[:, :, 0, :], lv[:, :, 0, :], lv_view(K, size)[:, :, 0, :], ALU.mult).then_inc(lv_ready, 1)

            def lv_drain(u, n):
                m = n % 2
                dve.wait_ge(filled[m], (A_M0 * u + 1 + n // 2) if m == 0 else (A_M1 * u + 2 + n // 2))
                dve.wait_ge(drained[1 - m], (A_M1 * u + 1 + n // 2) if m == 0 else (A_M0 * u + 1 + n // 2))
                nc.vector.memset(wait_pad[:], 0.0)
                nc.vector.copy_predicated(blocks(SC), level[:, n:n + 1, :].to_broadcast([P, BLK, P]),
                                          mixb(m)).then_inc(drained[m], 1)

            def a_unit(u):
                g = 4 * u
                nc.vector.tensor_copy(lb_now[:], lb_all[:, :, bass.ds(u, 1)]).then_inc(lb_copied, 1)
                evict(g, 0, T1).then_inc(tile_evicted, 1)
                dve.wait_ge(tile_evicted, g + 1)
                ts(arr(T2), arr(T1), -SAFE, None, ALU.max).then_inc(z_clamped, 1)
                dve.wait_ge(z_clamped, u + 1)
                ts(arr(T1), arr(T1), SAFE, 0.0, ALU.add, ALU.min).then_inc(z_under, 1)
                dve.wait_ge(z_loglb, u + 1)
                dve.wait_ge(z_under, u + 1)
                dve.wait_ge(lb_copied, u + 1)
                stt(out=arr(T1), in0=arr(T1), scalar=lb_now[:, 2, :], in1=arr(B), op0=ALU.mult,
                    op1=ALU.add).then_inc(z_sum, 1)
                dve.wait_ge(z_log, u + 1)
                dve.wait_ge(z_sum, u + 1)
                tt(arr(T1), arr(T1), arr(T3), ALU.subtract).then_inc(logf_ready, 1)
                dve.wait_ge(z_sig, u + 1)
                stt(out=arr(K), in0=arr(T2), scalar=lb_now[:, 1, :], in1=arr(K), op0=ALU.mult,
                    op1=ALU.mult).then_inc(k_ready, 1)
                dve.wait_ge(logf_ready, u + 1)
                for half in range(2):
                    cols = slice(half * HALF, half * HALF + HALF)
                    nc.vector.tensor_tensor_scan(arr(B)[:, cols], scan_mask[:], arr(T1)[:, cols], 0.0,
                                                 ALU.mult, ALU.add).then_inc(b_ready, 1)
                dve.wait_ge(b_ready, 2 * u + 2)
                dve.wait_ge(k_ready, u + 1)
                ends = blocks(B)[:, :, P - 1:P].to_broadcast([P, BLK, P])
                tt(blocks(T3), ends, blocks(B), ALU.subtract).then_inc(kd_diff, 1)
                silu_evict(g + 1, 1, 2 * u)
                lv_diff_of(u, 0)
                lv_diff_of(u, 1)
                silu_finish(2 * u, Q, A_DK ** -0.5)
                dve.wait_ge(silu_done, 2 * u + 1)
                dve.wait_ge(qe_exp, u + 1)
                tt(arr(QE), arr(QE), arr(Q), ALU.mult).then_inc(qe_ready, 1)
                dve.wait_ge(kd_exp, u + 1)
                tt(arr(T3), arr(T3), arr(K), ALU.mult).then_inc(kd_ready, 1)
                lv_mult(u, 0)
                dve.wait_ge(filled[1], A_M1 * u + 1)
                tt(blocks(SC), mixb(1), ident[:, None, :].to_broadcast([P, BLK, P]),
                   ALU.mult).then_inc(drained[1], 1)
                lv_mult(u, 1)
                evict(g + 2, 0, VT).then_inc(tile_evicted, 1)
                for n in range(NL):
                    if n + 2 < NL:
                        lv_diff_of(u, n + 2)
                    lv_drain(u, n)
                    if n == 3:
                        silu_evict(g + 3, 1, 2 * u + 1)
                    if n + 2 < NL:
                        lv_mult(u, n + 2)
                    if n == 4:
                        silu_finish(2 * u + 1, GATE, 1.0)
                dve.wait_ge(end_ready, u + 1)
                states(u, 1, P, ST, A_M1 * u + 6, lambda c: end_dec[:, c:c + 1])
                finish_y(u, u, 2 * u + 2, 0, A_M0 * u + 6, hgain_sb[:, 0:1])

            def finish_y(u, m, gate, n, o_drain, scale):
                dve.wait_ge(orms_ready, m + 1)
                dve.wait_ge(y_stored, 16 * u + 16)
                stt(out=arr(Y), in0=mix[n][:], scalar=scale, in1=arr(T1), op0=ALU.mult,
                    op1=ALU.mult).then_inc(drained[n], 1)
                dve.wait_ge(drained[n], o_drain)
                dve.wait_ge(silu_done, gate)
                tt(arr(Y), arr(Y), arr(GATE), ALU.mult).then_inc(y_ready, 1)

            with dve.Fori(0, A_HEADS) as u:
                a_unit(u)

            def b_block(i, p):
                nk = min(p + 1, B_BAND)
                w, m = nk * P, p % 2
                dve.wait_ge(filled[0], M0_B + B_M0 * i + 2 + p)
                if p >= 2:
                    dve.wait_ge(filled[1], M1_B + B_M1 * i + 2 * p - 3)
                stt(out=arr(BP[m])[:, 0:w], in0=mix[0][:, 0:w], scalar=B_DH ** -0.5,
                    in1=bias[:, 0:w][:, ::-1], op0=ALU.mult, op1=ALU.add).then_inc(drained[0], 1)
                dve.wait_ge(drained[0], M0_B + B_M0 * i + 2 + p)
                nc.vector.tensor_reduce(row_max[:, m, :], arr(BP[m])[:, 0:w], AX_X, ALU.max,
                                        negate=True).then_inc(p_max, 1)
                dve.wait_ge(p_exp, BLK * i + p + 1)
                nc.vector.reciprocal(row_inv[:, m, :], row_sum[:, m, :]).then_inc(p_inv, 1)
                dve.wait_ge(p_inv, BLK * i + p + 1)
                ts(arr(BP[m])[:, 0:w], arr(BP[m])[:, 0:w], row_inv[:, m, :], None,
                   ALU.mult).then_inc(p_ready, 1)

            def b_out(i, p):
                dve.wait_ge(filled[1], M1_B + B_M1 * i + 2 * p + 2)
                nc.vector.tensor_copy(blocks(Y)[:, p, :], mixb(1)[:, 5, :]).then_inc(drained[1], 1)

            def b_unit(i):
                g = TB + 4 * i
                for j, dst in enumerate((BQ, BK)):
                    evict(g + j, j, dst).then_inc(tile_evicted, 1)
                dve.wait_ge(bias_in, 16 * i + 16)
                nc.vector.memset(bias[0:P // 2, 0:P // 2], NEG_INF).then_inc(bias_ready, 1)
                nc.vector.memset(bias[P // 2:P, BAND - P // 2:BAND], NEG_INF).then_inc(bias_ready, 1)
                evict(g + 2, 0, VT).then_inc(tile_evicted, 1)
                dve.wait_ge(bias_ready, 2 * i + 2)
                dve.wait_ge(y_stored, 16 * (B0 + i) + 16)
                for n in range(BLK + 2):
                    if n >= 2:
                        b_out(i, n - 2)
                    if n < BLK:
                        b_block(i, n)
                    if n == 4:
                        silu_evict(g + 3, 1, 2 * A_HEADS + i)
                silu_finish(2 * A_HEADS + i, GATE, 1.0)
                dve.wait_ge(silu_done, 2 * A_HEADS + i + 1)
                dve.wait_ge(drained[1], M1_B + B_M1 * (i + 1))
                tt(arr(Y), arr(Y), arr(GATE), ALU.mult).then_inc(y_ready, 1)

            with dve.Fori(0, B_HEADS) as i:
                b_unit(i)

            def c_unit(i):
                g = TC + 3 * i
                heads = A_HEADS + i
                evict(g, 0, T1).then_inc(tile_evicted, 1)
                dve.wait_ge(tile_evicted, g + 1)
                tt(arr(T2), arr(T1), arr(CCOS), ALU.mult).then_inc(c_cos, 1)
                dve.wait_ge(filled[0], M0_C + C_M0 * i + 1)
                tt(arr(T3), mix[0][:], arr(CSIN), ALU.mult).then_inc(drained[0], 1)
                dve.wait_ge(c_cos, i + 1)
                dve.wait_ge(drained[0], M0_C + C_M0 * i + 1)
                tt(arr(CQK), arr(T2), arr(T3), ALU.add).then_inc(c_rot, 1)
                dve.wait_ge(c_rot, i + 1)
                dve.wait_ge(cdec_in, 16 * i + 16)
                tt(blocks(CQD)[0:C_DK], blocks(CQK)[0:C_DK],
                   dec[0:C_DK, None, P:2 * P].to_broadcast([C_DK, BLK, P]), ALU.mult).then_inc(c_qd, 1)
                evict(g + 1, 1, VT).then_inc(tile_evicted, 1)
                dve.wait_ge(filled[1], M1_C + C_M1 * i + 1)
                ts(arena[:, CKT, 0:BLK * C_DK].rearrange("p (c k) -> p c k", c=BLK),
                   mixb(1)[:, :, C_DK:P], dec[:, 2 * P:2 * P + 1], C_DK ** -0.5, ALU.mult,
                   ALU.mult).then_inc(drained[1], 1)
                dve.wait_ge(filled[1], M1_C + C_M1 * i + 2)
                tt(blocks(CSC), mixb(1), dec[:, None, 0:P].to_broadcast([P, BLK, P]),
                   ALU.mult).then_inc(drained[1], 1)
                states(heads, 0, C_DK, CST, M0_C + C_M0 * i + 3,
                       lambda c: dec[0:C_DK, 2 * P + 1:2 * P + 2])
                m = 2 * A_HEADS + B_HEADS + i
                silu_evict(g + 2, 0, m)
                silu_finish(m, GATE, 1.0)
                finish_y(C0 + i, heads, m + 1, 1, M1_C + C_M1 * i + 3, 1.0)

            dve.wait_ge(ctab_in, 48)
            with dve.Fori(0, C_HEADS) as i:
                c_unit(i)

            dve.wait_ge(w_used, NG * TO)
            for d in range(KB):
                dve.wait_ge(yl_in[d % 4], 16 * (d // 4 + 1))
                ts(mv_hi[:, d, :], arr(YS[d % 4]), 1.0, None, ALU.mult).then_inc(yl_hi, 1)
                dve.wait_ge(yl_hi, d + 1)
                tt(mv_lo[:, d, :], arr(YS[d % 4]), mv_hi[:, d, :].bitcast(F32),
                   ALU.subtract).then_inc(yl_lo, 1)

            def residual(c, pair):
                dve.wait_ge(w_used, NG * (TO + c) + NG)
                tt(arr(c), prj[pair][:], arr(c), ALU.add).then_inc(tile_evicted, 1)

            dve.wait_ge(xr_in[0], 16 * YS[0])
            dve.wait_ge(xr_in[1], 16 * (KB - YS[0]))
            with dve.Fori(0, KB // 2) as j:
                residual(2 * j, 1)
                residual(2 * j + 1, 0)
            dve.wait_ge(fin_rstd, 1)
            for c in range(KB):
                stt(out=arr(c), in0=arr(c), scalar=fgain_sb[:, c:c + 1], in1=rstd[:], op0=ALU.mult,
                    op1=ALU.mult).then_inc(out_ready, 1)


def layouts(x, w_in, norm_gain, lb_logits, hgrn_norm_gain, rel_bias, w_out, final_gain):
    sizes = [A_HEADS * A_DK] * 4 + [B_HEADS * B_DH] * 4 + [C_HEADS * C_DK] * 2 + [C_HEADS * P] * 2
    at = np.concatenate([[0], np.cumsum(sizes)])
    aq, af, ai, ag, bq, bk, bv, bg, cq, ck, cv, cg = [int(n) for n in at[:-1]]
    cols = []
    for h in range(A_HEADS):
        cols += [np.arange(s + P * h, s + P * h + P) for s in (af, aq, ai, ag)]
    for h in range(B_HEADS):
        cols += [np.arange(s + P * h, s + P * h + P) for s in (bq, bk, bv, bg)]
    for h in range(C_HEADS):
        cols += [np.arange(s + C_DK * h, s + C_DK * h + C_DK) for s in (cq, ck)]
        cols += [np.arange(s + P * h, s + P * h + P) for s in (cv, cg)]
    cols = np.concatenate(cols)

    def tiles(m):
        return m.reshape(NG, GRAN, P, -1, P).transpose(3, 2, 0, 1, 4)

    w = np.concatenate([tiles(w_in[0][:, cols]), tiles(w_out[0])])
    return {"xT": np.ascontiguousarray(x[0].T).reshape(KB, P, SEQ), "w": np.ascontiguousarray(w),
            "gain": np.ascontiguousarray(norm_gain[0].reshape(KB, P).T),
            "lbl": np.ascontiguousarray(lb_logits[0].reshape(A_HEADS, P).T),
            "hgain": np.ascontiguousarray(hgrn_norm_gain[0].reshape(P, 1)),
            "relb": np.ascontiguousarray(rel_bias[0]),
            "fgain": np.ascontiguousarray(final_gain.reshape(KB, P).T)}


def kernel(**inputs):
    import concourse.bacc as bacc
    from concourse.bass_utils import run_bass_kernel_spmd

    arrays = layouts(**{name: np.asarray(a) for name, a in inputs.items()})
    arrays.update(shape_tables())
    nc = bacc.Bacc("TRN2", target_bir_lowering=False, num_devices=1, dynamic_dma_scratch_size=1024)
    args = [nc.dram_tensor(f"in_{name}", a.shape, mybir.dt.from_np(a.dtype), kind="ExternalInput").ap()
            for name, a in arrays.items()]
    out = nc.dram_tensor("outT", (KB, P, SEQ), F32, kind="ExternalOutput").ap()
    build(nc, *args, out)
    r = run_bass_kernel_spmd(nc, [{f"in_{name}": a for name, a in arrays.items()}], core_ids=[0])
    got = np.asarray(r.results[0]["outT"])
    return np.ascontiguousarray(got.reshape(D_MODEL, SEQ).T).reshape(1, SEQ, D_MODEL)
```

```python
from contextlib import ExitStack

import numpy as np
import concourse.bass as bass
from concourse import mybir

F32 = mybir.dt.float32
F32R = mybir.dt.float32r
I8 = mybir.dt.int8
ALU = mybir.AluOpType
ACT = mybir.ActivationFunctionType
AX_X = mybir.AxisListType.X

P = 128
D_MODEL, SEQ = 2048, 1024
KB = D_MODEL // P
GRAN = 4
NG = KB // GRAN
BLK = SEQ // P
HALF = 512
EPS = 1e-6
NEG_INF = -1e30
SAFE = 40.0

A_HEADS, A_DK = 6, 128
B_HEADS, B_DH, B_BAND = 5, 128, 5
C_HEADS, C_DK = 5, 64
REL = 2 * 128 + 1
BAND = B_BAND * P
A0, B0, C0 = 0, A_HEADS, A_HEADS + B_HEADS
UNITS = A_HEADS + B_HEADS + C_HEADS
TA, TB = 0, 4 * A_HEADS
TC = TB + 4 * B_HEADS
TO = TC + 3 * C_HEADS
TILES = TO + D_MODEL // P
LEVELS = [64, 32, 16, 8, 4, 2, 1]
NL = len(LEVELS)
WIDE = 2

A_M0, A_M1 = 6, 7
B_M0, B_M1 = 1 + BLK, 2 * BLK
C_M0, C_M1 = 4, 3
M0_B, M1_B = A_HEADS * A_M0, A_HEADS * A_M1
M0_C, M1_C = M0_B + B_HEADS * B_M0, M1_B + B_HEADS * B_M1
M0_O = M0_C + C_HEADS * C_M0


def shape_tables():
    t = np.arange(P)
    ident = np.eye(P, dtype=np.float32)
    level = np.zeros((P, NL - WIDE, P), np.float32)
    for n, size in enumerate(LEVELS[WIDE:]):
        same = (t[:, None] // (2 * size)) == (t[None, :] // (2 * size))
        level[:, n] = same & ((t[:, None] // size) % 2 == 0) & ((t[None, :] // size) % 2 == 1)
    start = np.ones((P, HALF), np.float32)
    start[:, ::P] = 0
    swap = np.zeros((P, P), np.float32)
    half = C_DK // 2
    for base in (0, C_DK):
        for j in range(half):
            swap[base + half + j, base + j] = -1.0
            swap[base + j, base + half + j] = 1.0
    freq = np.float32(10000.0) ** (-np.linspace(0.0, 1.0, half, dtype=np.float32))
    ang = np.arange(SEQ, dtype=np.float32)[:, None] * freq[None, :].astype(np.float32)
    cos = np.tile(np.cos(ang).astype(np.float32).T, (4, 1))
    sin = np.tile(np.sin(ang).astype(np.float32).T, (4, 1))
    dec = np.zeros((C_HEADS, P, 2 * P + 2), np.float32)
    for h in range(C_HEADS):
        lg = np.log1p(-np.exp2(-5.0 - h))
        rel = t[None, :] - t[:, None]
        dec[h, :, 0:P] = np.where(rel >= 0, np.exp(lg * np.maximum(rel, 0)), 0.0)
        dec[h, :, P:2 * P] = np.exp(lg * (t + 1.0))[None, :]
        dec[h, :, 2 * P] = np.exp(lg * (P - 1 - t))
        dec[h, :, 2 * P + 1] = np.exp(lg * P)
    return {"ident": ident, "level": level, "start": start, "swap": swap,
            "rot": np.stack([cos, sin]), "dec": dec}


def build(nc, xT, w, gain, lbl, hgain, relb, fgain, ident_d, level_d, start_d, swap_d, rot_d, dec_d, outT):
    y_dram = nc.dram_tensor("y_scratch", (UNITS, P, SEQ), F32, kind="Internal").ap()
    rel_dram = nc.dram_tensor("rel_scratch", (B_HEADS, BAND + P), F32, kind="Internal").ap()

    with ExitStack() as ctx:
        def sb(name, shape, dt=F32):
            return ctx.enter_context(nc.sbuf_tensor(name, shape, dt))

        def sem(name):
            return ctx.enter_context(nc.semaphore(name))

        mv_hi = sb("mv_hi", [P, KB, SEQ], F32R)
        mv_lo = sb("mv_lo", [P, KB, SEQ], F32R)
        w_raw = [sb(f"w_raw{q}", [P, GRAN, P]) for q in range(NG)]
        w_hi = [sb(f"w_hi{q}", [P, GRAN, P], F32R) for q in range(NG)]
        w_lo = [sb(f"w_lo{q}", [P, GRAN, P], F32R) for q in range(NG)]
        arena = sb("arena", [P, 16, SEQ])
        rstd = sb("rstd", [P, SEQ])
        ident = sb("ident", [P, P])
        ones = sb("ones", [P, P])
        level = sb("level", [P, NL - WIDE, P], I8)
        gain_sb = sb("gain_sb", [P, KB])
        fgain_sb = sb("fgain_sb", [P, KB])
        hgain_sb = sb("hgain_sb", [P, 1])
        lb_all = sb("lb_all", [P, 4, A_HEADS])
        lb_now = sb("lb_now", [P, 4, 1])
        end_dec = sb("end_dec", [P, BLK])
        row_max = sb("row_max", [P, 2, 1])
        row_sum = sb("row_sum", [P, 2, 1])
        row_inv = sb("row_inv", [P, 2, 1])
        wait_pad = sb("wait_pad", [P, 1])
        eps_sb = sb("eps_sb", [P, 1])

        def arr(n):
            return arena[:, n, :]

        relrow = arena[0:B_HEADS, 7, 0:REL]

        level_f32 = arena[:, 8, 0:(NL - WIDE) * P].rearrange("p (l t) -> p l t", l=NL - WIDE)
        start_f32 = arena[:, 9, 0:HALF]

        def blocks(n):
            return arena[:, n, :].rearrange("p (c t) -> p c t", c=BLK)

        T1, T2, T3, GATE, VT, V, Y = range(7)
        Q, K, B, LV0, LV1, SC, ST, KDT, QE = range(7, 16)
        BQ, BK, BP0, BP1, BT0, BT1, BIAS = range(7, 14)
        CQK, CK, CQD, CSC, CST, CKT, CCOS, CSIN, CDEC = range(7, 16)
        LV = [LV0, LV1]
        bias = arena[:, BIAS, 0:BAND]
        BP, BT = [BP0, BP1], [BT0, BT1]
        swap = arena[:, CDEC, 512:512 + P]
        dec = arena[:, CDEC, 0:2 * P + 2]
        scan_mask = sb("scan_mask", [P, HALF], I8)

        prj = [ctx.enter_context(nc.psum_tensor(f"prj{n}", [P, SEQ], F32)) for n in range(2)]
        mix = [ctx.enter_context(nc.psum_tensor(f"mix{n}", [P, SEQ], F32)) for n in range(2)]

        def mixb(n):
            return mix[n][:, :].rearrange("p (c t) -> p c t", c=BLK)

        const_in = sem("const_in")
        gain_in = sem("gain_in")
        x_in = [sem(f"x_in{n}") for n in range(4)]
        w_in = [sem(f"w_in{n}") for n in range(NG)]
        w_hi_done = sem("w_hi_done")
        w_split = sem("w_split")
        w_used = sem("w_used")
        tile_evicted = sem("tile_evicted")
        half_done = sem("half_done")
        filled = [sem("mix0_filled"), sem("mix1_filled")]
        drained = [sem("mix0_drained"), sem("mix1_drained")]
        h_hi = sem("h_hi")
        ones_ready = sem("ones_ready")
        h_lo = sem("h_lo")
        sq_ready = sem("sq_ready")
        sq_added = sem("sq_added")
        ss_ready = sem("ss_ready")
        start_dve = sem("start_dve")
        lb_exp = sem("lb_exp")
        masks_ready = sem("masks_ready")
        rms_log = sem("rms_log")
        rstd_ready = sem("rstd_ready")
        rel_wide = sem("rel_wide")
        silu_clamped = sem("silu_clamped")
        silu_exp = sem("silu_exp")
        silu_log = sem("silu_log")
        silu_sig = sem("silu_sig")
        silu_done = sem("silu_done")
        z_ready = sem("z_ready")
        z_clamped = sem("z_clamped")
        z_exp = sem("z_exp")
        z_log = sem("z_log")
        z_sig = sem("z_sig")
        z_loglb = sem("z_loglb")
        z_under = sem("z_under")
        z_sum = sem("z_sum")
        logf_ready = sem("logf_ready")
        b_ready = sem("b_ready")
        k_ready = sem("k_ready")
        lb_copied = sem("lb_copied")
        lv_diff = sem("lv_diff")
        lv_exp = sem("lv_exp")
        lv_ready = sem("lv_ready")
        qe_exp = sem("qe_exp")
        qe_ready = sem("qe_ready")
        kd_diff = sem("kd_diff")
        kd_exp = sem("kd_exp")
        kd_ready = sem("kd_ready")
        end_ready = sem("end_ready")
        state_ready = sem("state_ready")
        osq_ready = sem("osq_ready")
        orms_ready = sem("orms_ready")
        y_ready = sem("y_ready")
        y_stored = sem("y_stored")
        bias_in = sem("bias_in")
        bias_ready = sem("bias_ready")
        p_max = sem("p_max")
        p_exp = sem("p_exp")
        p_inv = sem("p_inv")
        p_ready = sem("p_ready")
        ctab_in = sem("ctab_in")
        cdec_in = sem("cdec_in")
        c_zeroed = sem("c_zeroed")
        c_cos = sem("c_cos")
        c_rot = sem("c_rot")
        c_k = sem("c_k")
        c_qd = sem("c_qd")
        yl_in = [sem(f"yl_in{n}") for n in range(4)]
        yl_hi = sem("yl_hi")
        yl_lo = sem("yl_lo")
        xr_in = [sem(f"xr_in{n}") for n in range(2)]
        fin_log = sem("fin_log")
        fin_rstd = sem("fin_rstd")
        out_ready = sem("out_ready")
        out_stored = sem("out_stored")

        block = ctx.enter_context(nc.Block())

        XS = [T1, T2, T3, GATE]
        SQ = [VT, V]
        YS = [T3, CCOS, CSIN, VT]

        @block.sync
        def _(sp):
            def load_x(d):
                if d >= 4:
                    sp.wait_ge(h_lo, d - 3)
                    sp.wait_ge(sq_ready, d - 3)
                sp.dma_start(arr(XS[d % 4]), xT[d]).then_inc(x_in[d % 4], 16)

            def load_w(g, first=False):
                for q in range(NG):
                    if not first:
                        sp.wait_ge(w_split, g * NG + (q + 1 - NG))
                    sp.dma_start(w_raw[q][:], w[g, :, q]).then_inc(w_in[q], 16)

            sp.dma_start(gain_sb[:], gain).then_inc(gain_in, 16)
            load_x(0)
            load_x(1)
            load_w(0, first=True)
            for d in range(2, 4):
                load_x(d)
            sp.dma_start(ident[:], ident_d).then_inc(const_in, 16)
            sp.dma_start(level_f32, level_d).then_inc(const_in, 16)
            sp.dma_start(start_f32, start_d).then_inc(const_in, 16)
            sp.dma_start(fgain_sb[:], fgain).then_inc(const_in, 16)
            sp.dma_start(hgain_sb[:], hgain).then_inc(const_in, 16)
            sp.dma_start(lb_all[:, 3, :], lbl).then_inc(const_in, 16)
            sp.dma_start(relrow, relb).then_inc(const_in, 16)
            for d in range(4, 8):
                load_x(d)
            load_w(1)
            for d in range(8, KB):
                load_x(d)
            with sp.Fori(2, TILES) as g:
                load_w(g)
            for half in range(2):
                cols = slice(half * HALF, half * HALF + HALF)
                for c in range(KB):
                    sp.wait_ge(out_ready, half * KB + c + 1)
                    sp.dma_start(outT[c][:, cols], arr(c)[:, cols]).then_inc(out_stored, 16)
            sp.wait_ge(out_stored, 2 * 16 * KB)
            sp.wait_ge(y_stored, 16 * UNITS)

        @block.gpsimd
        def _(pool):
            nc.gpsimd.memset(ones[:], 1.0).then_inc(ones_ready, 1)
            nc.gpsimd.memset(eps_sb[:], EPS).then_inc(ones_ready, 1)
            pool.wait_ge(ones_ready, 1)

            def split(g, first=False):
                for q in range(NG):
                    pool.wait_ge(w_in[q], 16 * g + 16)
                    if not first:
                        pool.wait_ge(w_used, g * NG + (q + 1 - NG))
                    nc.gpsimd.tensor_tensor(w_hi[q][:], w_raw[q][:],
                                            ones[:, None, :].to_broadcast([P, GRAN, P]),
                                            ALU.mult).then_inc(w_hi_done, 1)
                    pool.wait_ge(w_hi_done, g * NG + q + 1)
                    nc.gpsimd.tensor_tensor(w_lo[q][:], w_raw[q][:], w_hi[q][:].bitcast(F32),
                                            ALU.subtract).then_inc(w_split, 1)

            split(0, first=True)
            with pool.Fori(1, TILES) as g:
                split(g)

        @block.tensor
        def _(pe):
            def nothing():
                pass

            def project(g, pair, free, stages, before=None):
                if free is not None:
                    pe.wait_ge(tile_evicted, free)
                for q in range(NG):
                    pe.wait_ge(w_split, g * NG + q + 1)
                    for kk in range(GRAN):
                        k = q * GRAN + kk
                        if before:
                            before(k)
                        for wt, mv in ((w_hi, mv_hi), (w_hi, mv_lo), (w_lo, mv_hi)):
                            for half in range(2):
                                cols = slice(half * HALF, half * HALF + HALF)
                                last = nc.tensor.matmul(
                                    prj[pair][:, cols], wt[q][:, kk, :], mv[:, k, cols],
                                    start=(k == 0 and wt is w_hi and mv is mv_hi),
                                    stop=(k == KB - 1 and wt is w_lo))
                    last.then_inc(w_used, 1)
                    stages[q]()

            def project_pair(g, pairs, ready, after_granule=nothing, before_last=nothing):
                for q in range(NG):
                    for kk in range(GRAN):
                        k = q * GRAN + kk
                        ready(k)
                        for t in range(2):
                            s = 2 * q + t
                            if k == KB - 1 and t == 1:
                                before_last()
                            if kk == 0:
                                pe.wait_ge(w_split, g * NG + s + 1)
                            for wt, mv in ((w_hi, mv_hi), (w_hi, mv_lo), (w_lo, mv_hi)):
                                for half in range(2):
                                    cols = slice(half * HALF, half * HALF + HALF)
                                    last = nc.tensor.matmul(
                                        prj[pairs[t]][:, cols], wt[s % NG][:, kk, :], mv[:, k, cols],
                                        start=(k == 0 and wt is w_hi and mv is mv_hi),
                                        stop=(k == KB - 1 and wt is w_lo))
                            if kk == GRAN - 1:
                                last.then_inc(w_used, 1)
                    if q == 0:
                        after_granule()

            def project_last(g, pair, free, between):
                pe.wait_ge(tile_evicted, free)
                for half in range(2):
                    cols = slice(half * HALF, half * HALF + HALF)
                    for k in range(KB):
                        q, kk = k // GRAN, k % GRAN
                        if kk == 0 and half == 0:
                            pe.wait_ge(w_split, g * NG + q + 1)
                        if half == 1 and k == 6:
                            between()
                        for wt, mv in ((w_hi, mv_hi), (w_hi, mv_lo), (w_lo, mv_hi)):
                            last = nc.tensor.matmul(
                                prj[pair][:, cols], wt[q][:, kk, :], mv[:, k, cols],
                                start=(k == 0 and wt is w_hi and mv is mv_hi),
                                stop=(k == KB - 1 and wt is w_lo))
                    last.then_inc(half_done, 1)

            def fill(n, before):
                pe.wait_ge(drained[n], before)

            def transposes(n, src, wait, value, before):
                pe.wait_ge(const_in, 112)
                pe.wait_ge(wait, value)
                fill(n, before)
                for c in range(BLK):
                    last = nc.tensor.transpose(mixb(n)[:, c, :], blocks(src)[:, c, :], ident[:])
                last.then_inc(filled[n], 1)

            def a_vtr(u):
                return transposes(0, VT, tile_evicted, 4 * u + 3, A_M0 * u + 4)

            def a_diag(u):
                def stage():
                    pe.wait_ge(silu_done, 2 * u + 1)
                    pe.wait_ge(k_ready, u + 1)
                    fill(1, A_M1 * u)
                    for c in range(BLK):
                        last = nc.tensor.matmul(mixb(1)[:, c, :], blocks(K)[:, c, :],
                                                blocks(Q)[:, c, :], start=True, stop=True)
                    last.then_inc(filled[1], 1)
                return stage

            def a_level(u, n):
                def stage():
                    m = n % 2
                    pe.wait_ge(lv_ready, 2 * (NL * u + n + 1))
                    fill(m, (A_M0 * u + n // 2) if m == 0 else (A_M1 * u + 1 + n // 2))
                    size = LEVELS[n]
                    for c in range(BLK):
                        if n < WIDE:
                            for early in range(0, P, 2 * size):
                                late = early + size
                                last = nc.tensor.matmul(
                                    mixb(m)[early:early + size, c, late:late + size],
                                    blocks(LV[n % 2])[:, c, early:early + size],
                                    blocks(LV[n % 2])[:, c, late:late + size], start=True, stop=True)
                        else:
                            last = nc.tensor.matmul(mixb(m)[:, c, :], blocks(LV[n % 2])[:, c, :],
                                                    blocks(LV[n % 2])[:, c, :], start=True, stop=True)
                    last.then_inc(filled[m], 1)
                return stage

            def a_kdtr(u):
                def stage():
                    transposes(1, T3, kd_ready, u + 1, A_M1 * u + 4)
                    a_vtr(u)
                return stage

            def a_state(u):
                def stage():
                    pe.wait_ge(drained[1], A_M1 * u + 5)
                    pe.wait_ge(drained[0], A_M0 * u + 5)
                    for c in range(BLK - 1):
                        last = nc.tensor.matmul(mixb(1)[:, c, :], blocks(KDT)[:, c, :],
                                                blocks(V)[:, c, :], start=True, stop=True)
                    last.then_inc(filled[1], 1)
                return stage

            def a_out(u):
                def stage():
                    pe.wait_ge(drained[1], A_M1 * u + 6)
                    pe.wait_ge(qe_ready, u + 1)
                    fill(0, A_M0 * u + 5)
                    for c in range(BLK):
                        last = nc.tensor.matmul(mixb(0)[:, c, :], blocks(V)[:, c, :],
                                                blocks(SC)[:, c, :], start=True, stop=(c == 0))
                        if c > 0:
                            last = nc.tensor.matmul(mixb(0)[:, c, :], blocks(ST)[:, c, :],
                                                    blocks(QE)[:, c, :], start=False, stop=True)
                    last.then_inc(filled[0], 1)
                return stage

            def sum_squares(n, value, before):
                def stage():
                    pe.wait_ge(osq_ready, value)
                    fill(n, before)
                    for half in range(2):
                        cols = slice(half * HALF, half * HALF + HALF)
                        last = nc.tensor.matmul(mix[n][:, cols], ones[:], arr(T2)[:, cols],
                                                start=True, stop=True)
                    last.then_inc(filled[n], 1)
                return stage

            def a_ss(u):
                return sum_squares(1, u + 1, A_M1 * u + 6)

            def b_scores(i, p):
                pe.wait_ge(tile_evicted, TB + 4 * i + 2)
                fill(0, M0_B + B_M0 * i + 1 + p)
                nk = min(p + 1, B_BAND)
                first = p + 1 - nk
                for lo in range(0, nk * P, HALF):
                    hi = min(nk * P, lo + HALF)
                    last = nc.tensor.matmul(mix[0][:, lo:hi], blocks(BQ)[:, p, :],
                                            arr(BK)[:, first * P + lo:first * P + hi],
                                            start=True, stop=True)
                last.then_inc(filled[0], 1)

            def b_ptr(i, p):
                pe.wait_ge(p_ready, BLK * i + p + 1)
                fill(1, M1_B + B_M1 * i + 2 * p)
                nk = min(p + 1, B_BAND)
                for j in range(nk):
                    last = nc.tensor.transpose(mixb(1)[:, j, :], blocks(BP[p % 2])[:, j, :], ident[:])
                last.then_inc(filled[1], 1)

            def b_pv(i, p):
                fill(1, M1_B + B_M1 * i + 2 * p + 1)
                nk = min(p + 1, B_BAND)
                for j in range(nk):
                    last = nc.tensor.matmul(mixb(1)[:, 5, :], blocks(V)[:, p + 1 - nk + j, :],
                                            blocks(BT[p % 2])[:, j, :], start=(j == 0),
                                            stop=(j == nk - 1))
                last.then_inc(filled[1], 1)

            def b_visit(i, n):
                def stage():
                    if n >= 2:
                        b_pv(i, n - 2)
                    if n < BLK:
                        b_scores(i, n)
                    if 1 <= n <= BLK:
                        b_ptr(i, n - 1)
                return stage

            def b_vtr(i):
                return lambda: transposes(0, VT, tile_evicted, TB + 4 * i + 3, M0_B + B_M0 * i)

            def c_swap(i):
                def stage():
                    pe.wait_ge(tile_evicted, TC + 3 * i + 1)
                    if isinstance(i, int) and i == 0:
                        pe.wait_ge(ctab_in, 48)
                    fill(0, M0_C + C_M0 * i)
                    for half in range(2):
                        cols = slice(half * HALF, half * HALF + HALF)
                        last = nc.tensor.matmul(mix[0][:, cols], swap, arr(T1)[:, cols],
                                                start=True, stop=True)
                    last.then_inc(filled[0], 1)
                return stage

            def c_ktr(i):
                return lambda: transposes(1, CQK, c_rot, i + 1, M1_C + C_M1 * i)

            def c_vtr(i):
                return lambda: transposes(0, VT, tile_evicted, TC + 3 * i + 2, M0_C + C_M0 * i + 1)

            def c_scores(i):
                def stage():
                    pe.wait_ge(c_k, i + 1)
                    pe.wait_ge(c_rot, i + 1)
                    fill(1, M1_C + C_M1 * i + 1)
                    for c in range(BLK):
                        last = nc.tensor.matmul(mixb(1)[:, c, :], blocks(CK)[:, c, :],
                                                blocks(CQK)[:, c, :], start=True, stop=True)
                    last.then_inc(filled[1], 1)
                return stage

            def c_state(i):
                def stage():
                    pe.wait_ge(drained[1], M1_C + C_M1 * i + 1)
                    fill(0, M0_C + C_M0 * i + 2)
                    kt = arena[:, CKT, 0:BLK * C_DK].rearrange("p (c k) -> p c k", c=BLK)
                    for c in range(BLK - 1):
                        last = nc.tensor.matmul(mixb(0)[0:C_DK, c, :], kt[:, c, :],
                                                blocks(V)[:, c, :], start=True, stop=True)
                    last.then_inc(filled[0], 1)
                return stage

            def c_out(i):
                def stage():
                    pe.wait_ge(drained[0], M0_C + C_M0 * i + 3)
                    pe.wait_ge(c_qd, i + 1)
                    fill(1, M1_C + C_M1 * i + 2)
                    for c in range(BLK):
                        last = nc.tensor.matmul(mixb(1)[:, c, :], blocks(V)[:, c, :],
                                                blocks(CSC)[:, c, :], start=True, stop=(c == 0))
                        if c > 0:
                            last = nc.tensor.matmul(mixb(1)[:, c, :], blocks(CST)[:, c, :],
                                                    blocks(CQD)[:, c, :], start=False, stop=True)
                    last.then_inc(filled[1], 1)
                return stage

            def c_ss(i):
                return sum_squares(0, A_HEADS + i + 1, M0_C + C_M0 * i + 3)

            def a_late(u):
                return [a_level(u, 5), a_level(u, 6), a_kdtr(u), a_state(u),
                        nothing, a_out(u), a_ss(u), nothing]

            def b_late(i):
                return [b_visit(i, 4), b_visit(i, 5), b_visit(i, 6), b_visit(i, 7),
                        b_visit(i, 8), b_visit(i, 9), nothing, nothing]

            def c_late(i):
                return [c_out(i), c_ss(i), nothing, nothing, nothing, nothing, nothing, nothing]

            none8 = [nothing] * 8

            def ones_product(cols):
                return nc.tensor.matmul(mix[0][:, cols], ones[:], rstd[:, cols], start=True, stop=True)

            def start_tiles():
                def input_ss():
                    pe.wait_ge(ones_ready, 1)
                    pe.wait_ge(sq_added, KB)
                    for half in range(2):
                        last = ones_product(slice(half * HALF, half * HALF + HALF))
                    last.then_inc(ss_ready, 1)
                project_pair(0, (0, 1), lambda k: pe.wait_ge(h_lo, k + 1), before_last=input_ss)
                pe.wait_ge(rms_log, 1)

            def a_unit(u, late, start=False):
                g = 4 * u
                if start:
                    start_tiles()
                else:
                    project(g, 0, g - 1, late[0:4])
                    project(g + 1, 1, g, late[4:8])
                project(g + 2, 0, g + 1, [nothing, nothing, a_diag(u), a_level(u, 0)])
                project(g + 3, 1, g + 2, [a_level(u, 1), a_level(u, 2), a_level(u, 3), a_level(u, 4)])

            def b_unit(i, late):
                g = TB + 4 * i
                project(g, 0, g - 1, late[0:4])
                project(g + 1, 1, g, late[4:8])
                project(g + 2, 0, g + 1, none8[0:4])
                project(g + 3, 1, g + 2, [b_vtr_visit(i), b_visit(i, 1), b_visit(i, 2), b_visit(i, 3)])

            def b_vtr_visit(i):
                def stage():
                    b_vtr(i)()
                    b_visit(i, 0)()
                return stage

            def c_unit(i, late):
                g = TC + 3 * i
                project(g, 0, g, late[0:4])
                project(g + 1, 1, g, [nothing, c_swap(i), nothing, nothing])
                project(g + 2, 0, g + 1, [c_vtr_k(i), c_scores(i), c_state(i), nothing])

            def c_vtr_k(i):
                def stage():
                    c_ktr(i)()
                    c_vtr(i)()
                return stage

            a_unit(0, none8, start=True)
            with pe.Fori(1, A_HEADS) as u:
                a_unit(u, a_late(u - 1))
            b_unit(0, a_late(A_HEADS - 1))
            with pe.Fori(1, B_HEADS) as i:
                b_unit(i, b_late(i - 1))
            project(TC, 0, TC - 1, b_late(B_HEADS - 1)[0:4])
            b_visit(B_HEADS - 1, 8)()
            b_visit(B_HEADS - 1, 9)()
            project(TC + 1, 1, TC, [nothing, c_swap(0), nothing, nothing])
            project(TC + 2, 0, TC + 1, [c_vtr_k(0), c_scores(0), c_state(0), nothing])
            with pe.Fori(1, C_HEADS) as i:
                c_unit(i, c_late(i - 1))
            c_out(C_HEADS - 1)()

            pe.wait_ge(tile_evicted, TO)
            project_pair(TO, (1, 0), lambda k: pe.wait_ge(yl_lo, k + 1), c_ss(C_HEADS - 1))
            with pe.Fori(1, KB // 2 - 1) as j:
                project(TO + 2 * j, 1, TO + 2 * j - 1, none8[0:4])
                project(TO + 2 * j + 1, 0, TO + 2 * j, none8[0:4])
            project(TILES - 2, 1, TILES - 3, none8[0:4])

            def output_ss(half):
                pe.wait_ge(sq_added, 2 * KB + half)
                ones_product(slice(half * HALF, half * HALF + HALF)).then_inc(ss_ready, 1)

            def first_output_ss():
                fill(0, M0_O)
                output_ss(0)

            project_last(TILES - 1, 0, TILES - 2, first_output_ss)
            output_ss(1)

        @block.scalar
        def _(act):
            def nothing():
                pass

            def exp(out, src, **kw):
                return nc.scalar.activation(out, src, ACT.Exp, **kw)

            def ln(out, src, **kw):
                return nc.scalar.activation(out, src, ACT.Ln, **kw)

            def inv_rms(src, dst, count, log_done):
                act.wait_ge(ones_ready, 2)
                ln(dst, src, scale=1.0 / count, bias=eps_sb[:, 0:1]).then_inc(*log_done[0:2])
                act.wait_ge(log_done[0], log_done[2])
                return exp(dst, dst, scale=-0.5)

            def sigmoid(m):
                act.wait_ge(silu_clamped, m + 1)
                exp(arr(T2), arr(T2), scale=-1.0).then_inc(silu_exp, 1)
                act.wait_ge(silu_exp, m + 1)
                ln(arr(T2), arr(T2), bias=1.0).then_inc(silu_log, 1)
                act.wait_ge(silu_log, m + 1)
                exp(arr(T2), arr(T2), scale=-1.0).then_inc(silu_sig, 1)

            def copy_v(fills):
                act.wait_ge(filled[0], fills)
                nc.scalar.activation(arr(V), mix[0][:], ACT.Copy).then_inc(drained[0], 1)

            def store_y(u):
                act.wait_ge(y_ready, u + 1)
                act.dma_start(y_dram[u], arr(Y)).then_inc(y_stored, 16)

            nc.scalar.preload_act_table_set("natural_log_exp_and_others")
            act.wait_ge(gain_in, 16)
            for d in range(KB):
                act.wait_ge(x_in[d % 4], 16 * (d // 4 + 1))
                nc.scalar.activation(mv_hi[:, d, :], arr(XS[d % 4]), ACT.Copy,
                                     scale=gain_sb[:, d:d + 1]).then_inc(h_hi, 1)
                if d >= 2:
                    act.wait_ge(sq_added, d - 1)
                nc.scalar.activation(arr(SQ[d % 2]), arr(XS[d % 4]), ACT.Square).then_inc(sq_ready, 1)
            act.wait_ge(start_dve, 1)
            exp(lb_all[:, 0, :], lb_all[:, 0, :]).then_inc(lb_exp, 1)
            act.wait_ge(rel_wide, 2)
            act.dma_start(rel_dram, arena[0:B_HEADS, Y, 0:BAND + P]).then_inc(y_stored, 16)
            act.wait_ge(ss_ready, 1)
            inv_rms(mix[0][:], rstd[:], D_MODEL, (rms_log, 1, 1)).then_inc(rstd_ready, 1)

            def a_unit(u):
                act.wait_ge(z_clamped, u + 1)
                exp(arr(T2), arr(T2), scale=-1.0).then_inc(z_exp, 1)
                act.wait_ge(z_exp, u + 1)
                ln(arr(T3), arr(T2), bias=1.0).then_inc(z_log, 1)
                act.wait_ge(lb_copied, u + 1)
                ln(arr(B), arr(T2), scale=lb_now[:, 0, :], bias=1.0).then_inc(z_loglb, 1)
                act.wait_ge(z_log, u + 1)
                exp(arr(K), arr(T3), scale=-1.0).then_inc(z_sig, 1)
                sigmoid(2 * u)
                act.wait_ge(b_ready, 2 * u + 2)
                exp(arr(QE), arr(B)).then_inc(qe_exp, 1)
                exp(end_dec[:, :], blocks(B)[:, :, P - 1]).then_inc(end_ready, 1)
                act.wait_ge(kd_diff, u + 1)
                exp(arr(T3), arr(T3)).then_inc(kd_exp, 1)
                for n in range(NL):
                    if n == NL - 1:
                        sigmoid(2 * u + 1)
                    act.wait_ge(lv_diff, 2 * (NL * u + n + 1))
                    exp(arr(LV[n % 2]), arr(LV[n % 2])).then_inc(lv_exp, 1)
                act.wait_ge(filled[1], A_M1 * u + 5)
                nc.scalar.activation(arr(KDT), mix[1][:], ACT.Copy).then_inc(drained[1], 1)
                copy_v(A_M0 * u + 5)
                norm(u, 2 * u + 2, 0, A_M0 * u + 6, 1, A_M1 * u + 7)
                store_y(u)

            def norm(m, gate, n_o, o_fills, n_ss, ss_fills):
                act.wait_ge(silu_done, gate)
                act.wait_ge(filled[n_o], o_fills)
                nc.scalar.activation(arr(T2), mix[n_o][:], ACT.Square).then_inc(osq_ready, 1)
                act.wait_ge(filled[n_ss], ss_fills)
                inv_rms(mix[n_ss][:], arr(T1), P, (drained[n_ss], 1, ss_fills)).then_inc(orms_ready, 1)

            with act.Fori(0, A_HEADS) as u:
                a_unit(u)

            def b_unit(i):
                act.wait_ge(drained[0], M0_B + B_M0 * i)
                act.dma_start(bias, bass.AP(tensor=rel_dram.tensor, offset=i * (BAND + P),
                                            ap=[[1, P], [1, BAND]])).then_inc(bias_in, 16)
                copy_v(M0_B + B_M0 * i + 1)
                for n in range(BLK + 2):
                    if n == 5:
                        sigmoid(2 * A_HEADS + i)
                    if n < BLK:
                        width = min(n + 1, B_BAND) * P
                        act.wait_ge(p_max, BLK * i + n + 1)
                        exp(arr(BP[n % 2])[:, 0:width], arr(BP[n % 2])[:, 0:width],
                            bias=row_max[:, n % 2, :], accum_out=row_sum[:, n % 2, :]).then_inc(p_exp, 1)
                    if 1 <= n <= BLK:
                        width = min(n, B_BAND) * P
                        act.wait_ge(filled[1], M1_B + B_M1 * i + 2 * n - 1)
                        nc.scalar.activation(arr(BT[(n - 1) % 2])[:, 0:width], mix[1][:, 0:width],
                                             ACT.Copy).then_inc(drained[1], 1)
                store_y(B0 + i)

            with act.Fori(0, B_HEADS) as i:
                b_unit(i)

            def c_unit(i, first_y=nothing, early_y=nothing, late_y=nothing):
                act.wait_ge(y_ready, C0 + i)
                act.dma_start(dec, dec_d[i]).then_inc(cdec_in, 16)
                act.wait_ge(c_rot, i + 1)
                act.wait_ge(c_zeroed, 2)
                nc.scalar.activation(arena[0:C_DK, CK, :], arena[C_DK:P, CQK, :], ACT.Copy,
                                     scale=C_DK ** -0.5).then_inc(c_k, 1)
                first_y()
                copy_v(M0_C + C_M0 * i + 2)
                early_y()
                sigmoid(2 * A_HEADS + B_HEADS + i)
                late_y()
                norm(A_HEADS + i, 2 * A_HEADS + B_HEADS + i + 1, 1, M1_C + C_M1 * i + 3, 0, M0_C + C_M0 * i + 4)

            def load_y(d):
                if d >= 4:
                    act.wait_ge(yl_lo, d - 3)
                act.dma_start(arr(YS[d % 4]), y_dram[d]).then_inc(yl_in[d % 4], 16)

            def y_hi(d, src):
                act.wait_ge(w_used, NG * (TO - 1) + d // GRAN + 1)
                nc.scalar.activation(mv_hi[:, d, :], src, ACT.Copy).then_inc(yl_hi, 1)

            def y_hi_loaded(d):
                act.wait_ge(yl_in[d % 4], 16 * (d // 4 + 1))
                y_hi(d, arr(YS[d % 4]))

            def first_y():
                act.wait_ge(y_stored, 16 * UNITS)
                for d in range(3):
                    load_y(d)

            def early_y():
                load_y(3)
                for d in range(8):
                    y_hi_loaded(d)
                    if d % 4 == 3:
                        for later in range(d + 1, d + 5):
                            load_y(later)

            def late_y():
                for d in range(8, KB - 1):
                    y_hi_loaded(d)
                    if d == 11:
                        for later in range(12, KB - 1):
                            load_y(later)

            act.wait_ge(p_ready, BLK * B_HEADS)
            act.dma_start(arr(CCOS), rot_d[0]).then_inc(ctab_in, 16)
            act.dma_start(arr(CSIN), rot_d[1]).then_inc(ctab_in, 16)
            act.dma_start(swap, swap_d).then_inc(ctab_in, 16)
            with act.Fori(0, C_HEADS - 1) as i:
                c_unit(i)
                store_y(C0 + i)
            c_unit(C_HEADS - 1, first_y, early_y, late_y)
            act.wait_ge(y_ready, UNITS)
            y_hi(KB - 1, arr(Y))

            act.wait_ge(yl_lo, KB)
            for c in range(KB):
                act.dma_start(arr(c), xT[c]).then_inc(xr_in[c // 8], 16)

            with act.Fori(0, KB - 1) as c:
                act.wait_ge(tile_evicted, TO + c + 1)
                act.wait_ge(sq_added, KB + c)
                nc.scalar.activation(rstd[:], arr(c), ACT.Square).then_inc(sq_ready, 1)
            act.wait_ge(sq_added, 2 * KB - 1)
            for half in range(2):
                cols = slice(half * HALF, half * HALF + HALF)
                act.wait_ge(tile_evicted, TILES + half)
                nc.scalar.activation(rstd[:, cols], arr(KB - 1)[:, cols], ACT.Square).then_inc(sq_ready, 1)
                act.wait_ge(ss_ready, 2 + half)
                inv_rms(mix[0][:, cols], rstd[:, cols], D_MODEL,
                        (fin_log, 1, half + 1)).then_inc(fin_rstd, 1)

        @block.vector
        def _(dve):
            tt = nc.vector.tensor_tensor
            ts = nc.vector.tensor_scalar
            stt = nc.vector.scalar_tensor_tensor

            def evict(g, pair, dst):
                dve.wait_ge(w_used, NG * g + NG)
                return tt(arr(dst), prj[pair][:], rstd[:], ALU.mult)

            def silu_evict(g, pair, m):
                evict(g, pair, T1).then_inc(tile_evicted, 1)
                dve.wait_ge(tile_evicted, g + 1)
                ts(arr(T2), arr(T1), -SAFE, None, ALU.max).then_inc(silu_clamped, 1)

            def silu_finish(m, dst, scale):
                dve.wait_ge(silu_sig, m + 1)
                stt(out=arr(dst), in0=arr(T1), scalar=scale, in1=arr(T2), op0=ALU.mult,
                    op1=ALU.mult).then_inc(silu_done, 1)

            def states(m, n, rows, st, fills, decay):
                dve.wait_ge(filled[n], fills)
                for c in range(BLK - 1):
                    cur = blocks(st)[0:rows, c + 1, :]
                    inc = mixb(n)[0:rows, c, :]
                    if c == 0:
                        new = nc.vector.tensor_copy(cur, inc)
                    else:
                        dve.wait_ge(state_ready, (BLK - 2) * m + c)
                        new = stt(out=cur, in0=blocks(st)[0:rows, c, :], scalar=decay(c), in1=inc,
                                  op0=ALU.mult, op1=ALU.add)
                    if c < BLK - 2:
                        new.then_inc(state_ready, 1)
                    else:
                        new.then_inc(drained[n], 1)

            dve.wait_ge(gain_in, 16)
            for d in range(KB):
                dve.wait_ge(x_in[d % 4], 16 * (d // 4 + 1))
                dve.wait_ge(h_hi, d + 1)
                stt(out=mv_lo[:, d, :], in0=arr(XS[d % 4]), scalar=gain_sb[:, d:d + 1],
                    in1=mv_hi[:, d, :].bitcast(F32), op0=ALU.mult, op1=ALU.subtract).then_inc(h_lo, 1)
                dve.wait_ge(sq_ready, d + 1)
                if d == 0:
                    nc.vector.tensor_copy(rstd[:], arr(SQ[0])).then_inc(sq_added, 1)
                else:
                    dve.wait_ge(sq_added, d)
                    tt(rstd[:], rstd[:], arr(SQ[d % 2]), ALU.add).then_inc(sq_added, 1)
            dve.wait_ge(const_in, 112)
            nc.vector.tensor_copy(level[:], level_f32).then_inc(masks_ready, 1)
            nc.vector.tensor_copy(scan_mask[:], start_f32).then_inc(masks_ready, 1)
            dve.wait_ge(masks_ready, 2)
            tt(lb_all[:, 0, :], lb_all[:, 3, :], lb_all[:, 3, :], ALU.subtract).then_inc(start_dve, 1)
            nc.vector.tensor_copy(arena[0:B_HEADS, Y, 0:REL - 2], relrow[:, 1:REL - 1]).then_inc(rel_wide, 1)
            nc.vector.tensor_copy(arena[0:B_HEADS, Y, REL - 2:BAND + P],
                                  relrow[:, REL - 1:REL].to_broadcast([B_HEADS, BAND + P - REL + 2])
                                  ).then_inc(rel_wide, 1)
            dve.wait_ge(lb_exp, 1)
            nc.vector.reciprocal(lb_all[:, 1, :], lb_all[:, 0, :]).then_inc(start_dve, 1)
            dve.wait_ge(start_dve, 2)
            tt(lb_all[:, 2, :], lb_all[:, 0, :], lb_all[:, 1, :], ALU.mult).then_inc(start_dve, 1)
            dve.wait_ge(start_dve, 3)
            tt(lb_all[:, 0, :], lb_all[:, 2, :], lb_all[:, 2, :], ALU.subtract).then_inc(start_dve, 1)
            dve.wait_ge(start_dve, 4)
            ts(lb_all[:, 1, :], lb_all[:, 0, :], -1.0, 1.0, ALU.mult, ALU.add).then_inc(start_dve, 1)
            ts(lb_all[:, 2, :], lb_all[:, 0, :], 0.0, None, ALU.is_equal).then_inc(start_dve, 1)
            dve.wait_ge(start_dve, 6)
            dve.wait_ge(y_stored, 16)
            dve.wait_ge(rstd_ready, 1)
            dve.wait_ge(w_used, 2 * NG)

            def lv_view(n, size):
                return arr(n).rearrange("p (a h t) -> p a h t", h=2, t=size)

            def lv_diff_of(u, n):
                size = LEVELS[n]
                if n >= 2:
                    m = n % 2
                    dve.wait_ge(filled[m], (A_M0 * u + n // 2) if m == 0 else (A_M1 * u + 1 + n // 2))
                b, lv = lv_view(B, size), lv_view(LV[n % 2], size)
                ref = b[:, :, 0, size - 1:size].to_broadcast([P, SEQ // (2 * size), size])
                tt(lv[:, :, 1, :], b[:, :, 1, :], ref, ALU.subtract).then_inc(lv_diff, 1)
                tt(lv[:, :, 0, :], ref, b[:, :, 0, :], ALU.subtract).then_inc(lv_diff, 1)

            def lv_mult(u, n):
                size = LEVELS[n]
                lv = lv_view(LV[n % 2], size)
                dve.wait_ge(lv_exp, NL * u + n + 1)
                tt(lv[:, :, 1, :], lv[:, :, 1, :], lv_view(Q, size)[:, :, 1, :], ALU.mult).then_inc(lv_ready, 1)
                tt(lv[:, :, 0, :], lv[:, :, 0, :], lv_view(K, size)[:, :, 0, :], ALU.mult).then_inc(lv_ready, 1)

            def lv_drain(u, n):
                m, size = n % 2, LEVELS[n]
                dve.wait_ge(filled[m], (A_M0 * u + 1 + n // 2) if m == 0 else (A_M1 * u + 2 + n // 2))
                dve.wait_ge(drained[1 - m], (A_M1 * u + 1 + n // 2) if m == 0 else (A_M0 * u + 1 + n // 2))
                if n < WIDE:
                    for early in range(0, P, 2 * size):
                        late = early + size
                        last = nc.vector.tensor_copy(blocks(SC)[early:early + size, :, late:late + size],
                                                     mixb(m)[early:early + size, :, late:late + size])
                    last.then_inc(drained[m], 1)
                    return
                nc.vector.memset(wait_pad[:], 0.0)
                nc.vector.copy_predicated(blocks(SC), level[:, n - WIDE:n - WIDE + 1, :].to_broadcast([P, BLK, P]),
                                          mixb(m)).then_inc(drained[m], 1)

            def a_unit(u):
                g = 4 * u
                nc.vector.tensor_copy(lb_now[:], lb_all[:, :, bass.ds(u, 1)]).then_inc(lb_copied, 1)
                evict(g, 0, T1).then_inc(tile_evicted, 1)
                dve.wait_ge(tile_evicted, g + 1)
                ts(arr(T2), arr(T1), -SAFE, None, ALU.max).then_inc(z_clamped, 1)
                dve.wait_ge(z_clamped, u + 1)
                ts(arr(T1), arr(T1), SAFE, 0.0, ALU.add, ALU.min).then_inc(z_under, 1)
                dve.wait_ge(z_loglb, u + 1)
                dve.wait_ge(z_under, u + 1)
                dve.wait_ge(lb_copied, u + 1)
                stt(out=arr(T1), in0=arr(T1), scalar=lb_now[:, 2, :], in1=arr(B), op0=ALU.mult,
                    op1=ALU.add).then_inc(z_sum, 1)
                dve.wait_ge(z_log, u + 1)
                dve.wait_ge(z_sum, u + 1)
                tt(arr(T1), arr(T1), arr(T3), ALU.subtract).then_inc(logf_ready, 1)
                dve.wait_ge(z_sig, u + 1)
                stt(out=arr(K), in0=arr(T2), scalar=lb_now[:, 1, :], in1=arr(K), op0=ALU.mult,
                    op1=ALU.mult).then_inc(k_ready, 1)
                dve.wait_ge(logf_ready, u + 1)
                for half in range(2):
                    cols = slice(half * HALF, half * HALF + HALF)
                    nc.vector.tensor_tensor_scan(arr(B)[:, cols], scan_mask[:], arr(T1)[:, cols], 0.0,
                                                 ALU.mult, ALU.add).then_inc(b_ready, 1)
                dve.wait_ge(b_ready, 2 * u + 2)
                dve.wait_ge(k_ready, u + 1)
                ends = blocks(B)[:, :, P - 1:P].to_broadcast([P, BLK, P])
                tt(blocks(T3), ends, blocks(B), ALU.subtract).then_inc(kd_diff, 1)
                silu_evict(g + 1, 1, 2 * u)
                lv_diff_of(u, 0)
                lv_diff_of(u, 1)
                silu_finish(2 * u, Q, A_DK ** -0.5)
                dve.wait_ge(silu_done, 2 * u + 1)
                dve.wait_ge(qe_exp, u + 1)
                tt(arr(QE), arr(QE), arr(Q), ALU.mult).then_inc(qe_ready, 1)
                dve.wait_ge(kd_exp, u + 1)
                tt(arr(T3), arr(T3), arr(K), ALU.mult).then_inc(kd_ready, 1)
                lv_mult(u, 0)
                dve.wait_ge(filled[1], A_M1 * u + 1)
                tt(blocks(SC), mixb(1), ident[:, None, :].to_broadcast([P, BLK, P]),
                   ALU.mult).then_inc(drained[1], 1)
                lv_mult(u, 1)
                evict(g + 2, 0, VT).then_inc(tile_evicted, 1)
                for n in range(NL):
                    if n + 2 < NL:
                        lv_diff_of(u, n + 2)
                    lv_drain(u, n)
                    if n == 3:
                        silu_evict(g + 3, 1, 2 * u + 1)
                    if n + 2 < NL:
                        lv_mult(u, n + 2)
                    if n == 4:
                        silu_finish(2 * u + 1, GATE, 1.0)
                dve.wait_ge(end_ready, u + 1)
                states(u, 1, P, ST, A_M1 * u + 6, lambda c: end_dec[:, c:c + 1])
                finish_y(u, u, 2 * u + 2, 0, A_M0 * u + 6, hgain_sb[:, 0:1])

            def finish_y(u, m, gate, n, o_drain, scale):
                dve.wait_ge(orms_ready, m + 1)
                dve.wait_ge(y_stored, 16 * u + 16)
                stt(out=arr(Y), in0=mix[n][:], scalar=scale, in1=arr(T1), op0=ALU.mult,
                    op1=ALU.mult).then_inc(drained[n], 1)
                dve.wait_ge(drained[n], o_drain)
                dve.wait_ge(silu_done, gate)
                tt(arr(Y), arr(Y), arr(GATE), ALU.mult).then_inc(y_ready, 1)

            with dve.Fori(0, A_HEADS) as u:
                a_unit(u)

            def b_block(i, p):
                nk = min(p + 1, B_BAND)
                w, m = nk * P, p % 2
                dve.wait_ge(filled[0], M0_B + B_M0 * i + 2 + p)
                if p >= 2:
                    dve.wait_ge(filled[1], M1_B + B_M1 * i + 2 * p - 3)
                stt(out=arr(BP[m])[:, 0:w], in0=mix[0][:, 0:w], scalar=B_DH ** -0.5,
                    in1=bias[:, 0:w][:, ::-1], op0=ALU.mult, op1=ALU.add).then_inc(drained[0], 1)
                dve.wait_ge(drained[0], M0_B + B_M0 * i + 2 + p)
                nc.vector.tensor_reduce(row_max[:, m, :], arr(BP[m])[:, 0:w], AX_X, ALU.max,
                                        negate=True).then_inc(p_max, 1)
                dve.wait_ge(p_exp, BLK * i + p + 1)
                nc.vector.reciprocal(row_inv[:, m, :], row_sum[:, m, :]).then_inc(p_inv, 1)
                dve.wait_ge(p_inv, BLK * i + p + 1)
                ts(arr(BP[m])[:, 0:w], arr(BP[m])[:, 0:w], row_inv[:, m, :], None,
                   ALU.mult).then_inc(p_ready, 1)

            def b_out(i, p):
                dve.wait_ge(filled[1], M1_B + B_M1 * i + 2 * p + 2)
                nc.vector.tensor_copy(blocks(Y)[:, p, :], mixb(1)[:, 5, :]).then_inc(drained[1], 1)

            def b_unit(i):
                g = TB + 4 * i
                for j, dst in enumerate((BQ, BK)):
                    evict(g + j, j, dst).then_inc(tile_evicted, 1)
                dve.wait_ge(bias_in, 16 * i + 16)
                nc.vector.memset(bias[0:P // 2, 0:P // 2], NEG_INF).then_inc(bias_ready, 1)
                nc.vector.memset(bias[P // 2:P, BAND - P // 2:BAND], NEG_INF).then_inc(bias_ready, 1)
                evict(g + 2, 0, VT).then_inc(tile_evicted, 1)
                dve.wait_ge(bias_ready, 2 * i + 2)
                dve.wait_ge(y_stored, 16 * (B0 + i) + 16)
                for n in range(BLK + 2):
                    if n >= 2:
                        b_out(i, n - 2)
                    if n < BLK:
                        b_block(i, n)
                    if n == 4:
                        silu_evict(g + 3, 1, 2 * A_HEADS + i)
                silu_finish(2 * A_HEADS + i, GATE, 1.0)
                dve.wait_ge(silu_done, 2 * A_HEADS + i + 1)
                dve.wait_ge(drained[1], M1_B + B_M1 * (i + 1))
                tt(arr(Y), arr(Y), arr(GATE), ALU.mult).then_inc(y_ready, 1)

            with dve.Fori(0, B_HEADS) as i:
                b_unit(i)

            def y_lo(d, src):
                dve.wait_ge(yl_hi, d + 1)
                tt(mv_lo[:, d, :], src, mv_hi[:, d, :].bitcast(F32), ALU.subtract).then_inc(yl_lo, 1)

            def y_lo_loaded(first, end):
                for d in range(first, end):
                    dve.wait_ge(yl_in[d % 4], 16 * (d // 4 + 1))
                    y_lo(d, arr(YS[d % 4]))

            def c_unit(i, last=False):
                g = TC + 3 * i
                heads = A_HEADS + i
                evict(g, 0, T1).then_inc(tile_evicted, 1)
                dve.wait_ge(tile_evicted, g + 1)
                tt(arr(T2), arr(T1), arr(CCOS), ALU.mult).then_inc(c_cos, 1)
                dve.wait_ge(filled[0], M0_C + C_M0 * i + 1)
                tt(arr(T3), mix[0][:], arr(CSIN), ALU.mult).then_inc(drained[0], 1)
                dve.wait_ge(c_cos, i + 1)
                dve.wait_ge(drained[0], M0_C + C_M0 * i + 1)
                tt(arr(CQK), arr(T2), arr(T3), ALU.add).then_inc(c_rot, 1)
                dve.wait_ge(c_rot, i + 1)
                dve.wait_ge(cdec_in, 16 * i + 16)
                tt(blocks(CQD), blocks(CQK), dec[:, None, P:2 * P].to_broadcast([P, BLK, P]),
                   ALU.mult).then_inc(c_qd, 1)
                evict(g + 1, 1, VT).then_inc(tile_evicted, 1)
                dve.wait_ge(filled[1], M1_C + C_M1 * i + 1)
                ts(arena[:, CKT, 0:BLK * C_DK].rearrange("p (c k) -> p c k", c=BLK),
                   mixb(1)[:, :, C_DK:P], dec[:, 2 * P:2 * P + 1], C_DK ** -0.5, ALU.mult,
                   ALU.mult).then_inc(drained[1], 1)
                dve.wait_ge(filled[1], M1_C + C_M1 * i + 2)
                tt(blocks(CSC), mixb(1), dec[:, None, 0:P].to_broadcast([P, BLK, P]),
                   ALU.mult).then_inc(drained[1], 1)
                if last:
                    y_lo_loaded(0, 4)
                states(heads, 0, C_DK, CST, M0_C + C_M0 * i + 3,
                       lambda c: dec[0:C_DK, 2 * P + 1:2 * P + 2])
                m = 2 * A_HEADS + B_HEADS + i
                if last:
                    y_lo_loaded(4, 8)
                silu_evict(g + 2, 0, m)
                silu_finish(m, GATE, 1.0)
                if last:
                    y_lo_loaded(8, KB - 1)
                finish_y(C0 + i, heads, m + 1, 1, M1_C + C_M1 * i + 3, 1.0)

            nc.vector.memset(arena[C_DK:P, CK, :], 0.0).then_inc(c_zeroed, 1)
            nc.vector.memset(arena[C_DK:P, CST, :], 0.0).then_inc(c_zeroed, 1)
            dve.wait_ge(ctab_in, 48)
            with dve.Fori(0, C_HEADS - 1) as i:
                c_unit(i)
            c_unit(C_HEADS - 1, last=True)
            dve.wait_ge(y_ready, UNITS)
            y_lo(KB - 1, arr(Y))

            def residual(c, pair, cols=slice(0, SEQ)):
                return tt(arr(c)[:, cols], prj[pair][:, cols], arr(c)[:, cols],
                          ALU.add).then_inc(tile_evicted, 1)

            def add_squares(c):
                dve.wait_ge(sq_ready, KB + c + 1)
                dve.wait_ge(sq_added, KB + c)
                tt(mix[1][:], mix[1][:], rstd[:], ALU.add).then_inc(sq_added, 1)

            def scale_half(half):
                cols = slice(half * HALF, half * HALF + HALF)
                dve.wait_ge(fin_rstd, half + 1)
                for c in range(KB):
                    stt(out=arr(c)[:, cols], in0=arr(c)[:, cols], scalar=fgain_sb[:, c:c + 1],
                        in1=rstd[:, cols], op0=ALU.mult, op1=ALU.mult).then_inc(out_ready, 1)

            dve.wait_ge(w_used, NG * (TO + 2))
            dve.wait_ge(xr_in[0], 16 * 8)
            residual(0, 1)
            residual(1, 0)
            dve.wait_ge(sq_ready, KB + 1)
            nc.vector.tensor_copy(mix[1][:], rstd[:]).then_inc(sq_added, 1)
            add_squares(1)
            dve.wait_ge(xr_in[1], 16 * 8)
            with dve.Fori(1, KB // 2 - 1) as j:
                for c, pair in ((2 * j, 1), (2 * j + 1, 0)):
                    dve.wait_ge(w_used, NG * (TO + c) + NG)
                    residual(c, pair)
                    add_squares(c)
            dve.wait_ge(w_used, NG * (TILES - 1))
            residual(KB - 2, 1)
            add_squares(KB - 2)
            for half in range(2):
                cols = slice(half * HALF, half * HALF + HALF)
                dve.wait_ge(half_done, half + 1)
                residual(KB - 1, 0, cols)
                dve.wait_ge(sq_ready, 2 * KB + half)
                dve.wait_ge(sq_added, 2 * KB - 1)
                tt(rstd[:, cols], mix[1][:, cols], rstd[:, cols], ALU.add).then_inc(sq_added, 1)
                if half == 1:
                    scale_half(0)
            scale_half(1)


def layouts(x, w_in, norm_gain, lb_logits, hgrn_norm_gain, rel_bias, w_out, final_gain):
    sizes = [A_HEADS * A_DK] * 4 + [B_HEADS * B_DH] * 4 + [C_HEADS * C_DK] * 2 + [C_HEADS * P] * 2
    at = np.concatenate([[0], np.cumsum(sizes)])
    aq, af, ai, ag, bq, bk, bv, bg, cq, ck, cv, cg = [int(n) for n in at[:-1]]
    cols = []
    for h in range(A_HEADS):
        cols += [np.arange(s + P * h, s + P * h + P) for s in (af, aq, ai, ag)]
    for h in range(B_HEADS):
        cols += [np.arange(s + P * h, s + P * h + P) for s in (bq, bk, bv, bg)]
    for h in range(C_HEADS):
        cols += [np.arange(s + C_DK * h, s + C_DK * h + C_DK) for s in (cq, ck)]
        cols += [np.arange(s + P * h, s + P * h + P) for s in (cv, cg)]
    cols = np.concatenate(cols)

    def tiles(m):
        return m.reshape(NG, GRAN, P, -1, P).transpose(3, 2, 0, 1, 4)

    w = np.concatenate([tiles(w_in[0][:, cols]), tiles(w_out[0])])
    for g in (0, TO):
        both = w[g:g + 2].transpose(2, 0, 1, 3, 4).reshape(2, NG, P, GRAN, P)
        w[g:g + 2] = both.transpose(0, 2, 1, 3, 4)
    return {"xT": np.ascontiguousarray(x[0].T).reshape(KB, P, SEQ), "w": np.ascontiguousarray(w),
            "gain": np.ascontiguousarray(norm_gain[0].reshape(KB, P).T),
            "lbl": np.ascontiguousarray(lb_logits[0].reshape(A_HEADS, P).T),
            "hgain": np.ascontiguousarray(hgrn_norm_gain[0].reshape(P, 1)),
            "relb": np.ascontiguousarray(rel_bias[0]),
            "fgain": np.ascontiguousarray(final_gain.reshape(KB, P).T)}


def kernel(**inputs):
    import concourse.bacc as bacc
    from concourse.bass_utils import run_bass_kernel_spmd

    arrays = layouts(**{name: np.asarray(a) for name, a in inputs.items()})
    arrays.update(shape_tables())
    nc = bacc.Bacc("TRN2", target_bir_lowering=False, num_devices=1, dynamic_dma_scratch_size=1024)
    args = [nc.dram_tensor(f"in_{name}", a.shape, mybir.dt.from_np(a.dtype), kind="ExternalInput").ap()
            for name, a in arrays.items()]
    out = nc.dram_tensor("outT", (KB, P, SEQ), F32, kind="ExternalOutput").ap()
    build(nc, *args, out)
    r = run_bass_kernel_spmd(nc, [{f"in_{name}": a for name, a in arrays.items()}], core_ids=[0])
    got = np.asarray(r.results[0]["outT"])
    return np.ascontiguousarray(got.reshape(D_MODEL, SEQ).T).reshape(1, SEQ, D_MODEL)
```

```python
from contextlib import ExitStack

import numpy as np
import concourse.bass as bass
from concourse import mybir

F32 = mybir.dt.float32
F32R = mybir.dt.float32r
I8 = mybir.dt.int8
ALU = mybir.AluOpType
ACT = mybir.ActivationFunctionType
AX_X = mybir.AxisListType.X

P = 128
D_MODEL, SEQ = 2048, 1024
KB = D_MODEL // P
GRAN = 4
NG = KB // GRAN
RAW = 2
BLK = SEQ // P
HALF = 512
EPS = 1e-6
NEG_INF = -1e30
SAFE = 40.0

A_HEADS, A_DK = 6, 128
B_HEADS, B_DH, B_BAND = 5, 128, 5
C_HEADS, C_DK = 5, 64
REL = 2 * 128 + 1
BAND = B_BAND * P
B0, C0 = A_HEADS, A_HEADS + B_HEADS
UNITS = A_HEADS + B_HEADS + C_HEADS
TB = 4 * A_HEADS
TC = TB + 4 * B_HEADS
TO = TC + 3 * C_HEADS
TILES = TO + D_MODEL // P
LEVELS = [64, 32, 16, 8, 4, 2, 1]
NL = len(LEVELS)
NM = NL - 1
WIDE = 2

A_M0, A_M1 = 6, 7
A_PARTS = 5
B_M0, B_M1 = 1 + BLK, 2 * BLK
C_M0, C_M1 = 3, 3
M0_B, M1_B = A_HEADS * A_M0, A_HEADS * A_M1
M0_C, M1_C = M0_B + B_HEADS * B_M0, M1_B + B_HEADS * B_M1
PARTS_C = A_HEADS * A_PARTS
M0_O = M0_C + C_HEADS * C_M0


def shape_tables():
    t = np.arange(P)
    ident = np.eye(P, dtype=np.float32)
    level = np.zeros((P, NL - WIDE, P), np.float32)
    for n, size in enumerate(LEVELS[WIDE:]):
        same = (t[:, None] // (2 * size)) == (t[None, :] // (2 * size))
        level[:, n] = same & ((t[:, None] // size) % 2 == 0) & ((t[None, :] // size) % 2 == 1)
    start = np.ones((P, HALF), np.float32)
    start[:, ::P] = 0
    half = C_DK // 2
    freq = np.float32(10000.0) ** (-np.linspace(0.0, 1.0, half, dtype=np.float32))
    ang = np.arange(SEQ, dtype=np.float32)[:, None] * freq[None, :].astype(np.float32)
    cos = np.tile(np.cos(ang).astype(np.float32).T, (4, 1))
    sin = np.tile(np.sin(ang).astype(np.float32).T, (4, 1))
    dec = np.zeros((C_HEADS, P, 2 * P + 2), np.float32)
    for h in range(C_HEADS):
        lg = np.log1p(-np.exp2(-5.0 - h))
        rel = t[None, :] - t[:, None]
        dec[h, :, 0:P] = np.where(rel >= 0, np.exp(lg * np.maximum(rel, 0)), 0.0)
        dec[h, :, P:2 * P] = np.exp(lg * (t + 1.0))[None, :]
        dec[h, :, 2 * P] = np.exp(lg * (P - 1 - t))
        dec[h, :, 2 * P + 1] = np.exp(lg * P)
    return {"ident": ident, "level": level, "start": start,
            "rot": np.stack([cos, sin]), "dec": dec}


def build(nc, xT, w, gain, lbl, hgain, relb, fgain, ident_d, level_d, start_d, rot_d, dec_d, outT):
    y_dram = nc.dram_tensor("y_scratch", (UNITS, P, SEQ), F32, kind="Internal").ap()
    rel_dram = nc.dram_tensor("rel_scratch", (B_HEADS, BAND + P), F32, kind="Internal").ap()

    with ExitStack() as ctx:
        def sb(name, shape, dt=F32):
            return ctx.enter_context(nc.sbuf_tensor(name, shape, dt))

        def sem(name):
            return ctx.enter_context(nc.semaphore(name))

        mv_hi = sb("mv_hi", [P, KB, SEQ], F32R)
        mv_lo = sb("mv_lo", [P, KB, SEQ], F32R)
        w_raw = [sb(f"w_raw{q}", [P, GRAN, P]) for q in range(RAW)]
        w_hi = [sb(f"w_hi{q}", [P, GRAN, P], F32R) for q in range(NG)]
        w_lo = [sb(f"w_lo{q}", [P, GRAN, P], F32R) for q in range(NG)]
        arena = sb("arena", [P, 16, SEQ])
        rstd = sb("rstd", [P, SEQ])
        ident = sb("ident", [P, P])
        ones = sb("ones", [P, P], F32R)
        part_hi = sb("part_hi", [P, HALF], F32R)
        part_lo = sb("part_lo", [P, HALF], F32R)
        level = sb("level", [P, NL - WIDE, P], I8)
        gain_sb = sb("gain_sb", [P, KB])
        fgain_sb = sb("fgain_sb", [P, KB])
        hgain_sb = sb("hgain_sb", [P, 1])
        lb_all = sb("lb_all", [P, 4, A_HEADS])
        lb_now = sb("lb_now", [P, 4, 1])
        end_dec = sb("end_dec", [P, BLK])
        row_max = sb("row_max", [P, 2, 1])
        row_sum = sb("row_sum", [P, 2, 1])
        row_inv = sb("row_inv", [P, 2, 1])
        wait_pad = sb("wait_pad", [P, 1])
        eps_sb = sb("eps_sb", [P, 1])

        def arr(n):
            return arena[:, n, :]

        relrow = arena[0:B_HEADS, 7, 0:REL]

        level_f32 = arena[:, 8, 0:(NL - WIDE) * P].rearrange("p (l t) -> p l t", l=NL - WIDE)
        start_f32 = arena[:, 9, 0:HALF]
        ones_f32 = arena[:, 10, 0:P]

        def blocks(n):
            return arena[:, n, :].rearrange("p (c t) -> p c t", c=BLK)

        T1, T2, T3, GATE, VT, V, Y = range(7)
        Q, K, B, LV0, LV1, SC, ST, KDT, QE = range(7, 16)
        BQ, BK, BP0, BP1, BT0, BT1, BIAS = range(7, 14)
        CQK, CK, CQD, CSC, CST, CKT, CCOS, CSIN, CDEC = range(7, 16)
        LV = [LV0, LV1]
        bias = arena[:, BIAS, 0:BAND]
        BP, BT = [BP0, BP1], [BT0, BT1]
        dec = arena[:, CDEC, 0:2 * P + 2]
        scan_mask = sb("scan_mask", [P, HALF], I8)

        prj = [ctx.enter_context(nc.psum_tensor(f"prj{n}", [P, SEQ], F32)) for n in range(2)]
        mix = [ctx.enter_context(nc.psum_tensor(f"mix{n}", [P, SEQ], F32)) for n in range(2)]

        def mixb(n):
            return mix[n][:, :].rearrange("p (c t) -> p c t", c=BLK)

        const_in = sem("const_in")
        gain_in = sem("gain_in")
        x_in = [sem(f"x_in{n}") for n in range(4)]
        w_in = [sem(f"w_in{n}") for n in range(NG)]
        w_hi_done = sem("w_hi_done")
        w_split = sem("w_split")
        w_used = sem("w_used")
        tile_evicted = sem("tile_evicted")
        half_done = sem("half_done")
        filled = [sem("mix0_filled"), sem("mix1_filled")]
        drained = [sem("mix0_drained"), sem("mix1_drained")]
        h_hi = sem("h_hi")
        ones_ready = sem("ones_ready")
        h_lo = sem("h_lo")
        sq_ready = sem("sq_ready")
        sq_added = sem("sq_added")
        ss_ready = sem("ss_ready")
        start_dve = sem("start_dve")
        lb_exp = sem("lb_exp")
        masks_ready = sem("masks_ready")
        rms_log = sem("rms_log")
        rstd_ready = sem("rstd_ready")
        rel_wide = sem("rel_wide")
        silu_clamped = sem("silu_clamped")
        silu_exp = sem("silu_exp")
        silu_log = sem("silu_log")
        silu_sig = sem("silu_sig")
        silu_done = sem("silu_done")
        z_clamped = sem("z_clamped")
        z_exp = sem("z_exp")
        z_log = sem("z_log")
        z_sig = sem("z_sig")
        z_loglb = sem("z_loglb")
        z_under = sem("z_under")
        z_sum = sem("z_sum")
        logf_ready = sem("logf_ready")
        b_ready = sem("b_ready")
        k_ready = sem("k_ready")
        lb_copied = sem("lb_copied")
        near_diff = sem("near_diff")
        near_exp = sem("near_exp")
        near_prod = sem("near_prod")
        lv_diff = sem("lv_diff")
        lv_exp = sem("lv_exp")
        lv_ready = sem("lv_ready")
        qe_exp = sem("qe_exp")
        qe_ready = sem("qe_ready")
        kd_diff = sem("kd_diff")
        kd_exp = sem("kd_exp")
        kd_ready = sem("kd_ready")
        end_ready = sem("end_ready")
        state_ready = sem("state_ready")
        parts_hi = sem("parts_hi")
        parts_split = sem("parts_split")
        first_part_used = sem("first_part_used")
        diag_prod = sem("diag_prod")
        osq_ready = sem("osq_ready")
        orms_ready = sem("orms_ready")
        y_ready = sem("y_ready")
        y_stored = sem("y_stored")
        bias_in = sem("bias_in")
        bias_ready = sem("bias_ready")
        p_max = sem("p_max")
        p_exp = sem("p_exp")
        p_inv = sem("p_inv")
        p_ready = sem("p_ready")
        ctab_in = sem("ctab_in")
        cdec_in = sem("cdec_in")
        c_zeroed = sem("c_zeroed")
        c_partner = sem("c_partner")
        c_cos = sem("c_cos")
        c_sin = sem("c_sin")
        c_rot = sem("c_rot")
        c_k = sem("c_k")
        c_qd = sem("c_qd")
        yl_in = [sem(f"yl_in{n}") for n in range(4)]
        yl_hi = sem("yl_hi")
        yl_lo = sem("yl_lo")
        xr_in = [sem(f"xr_in{n}") for n in range(4)]
        fin_log = sem("fin_log")
        fin_rstd = sem("fin_rstd")
        out_ready = sem("out_ready")
        out_stored = sem("out_stored")

        block = ctx.enter_context(nc.Block())

        XS = [T1, T2, T3, GATE]
        SQ = [VT, V]
        YS = [T3, CCOS, CSIN, VT]

        @block.sync
        def _(sp):
            def load_x(d):
                if d >= 4:
                    sp.wait_ge(h_lo, d - 3)
                    sp.wait_ge(sq_ready, d - 3)
                sp.dma_start(arr(XS[d % 4]), xT[d]).then_inc(x_in[d % 4], 16)

            def load_w(g):
                for q in range(NG):
                    sp.wait_ge(w_split, g * NG + (q + 1 - RAW))
                    sp.dma_start(w_raw[q % RAW][:], w[g, :, q]).then_inc(w_in[q], 16)

            def load_first_w(s):
                if s >= RAW:
                    sp.wait_ge(w_split, s + 1 - RAW)
                sp.dma_start(w_raw[s % RAW][:], w[s // NG, :, s % NG]).then_inc(w_in[s % NG], 16)

            sp.dma_start(gain_sb[:], gain).then_inc(gain_in, 16)
            load_first_w(0)
            load_x(0)
            load_first_w(1)
            load_x(1)
            load_x(2)
            load_first_w(2)
            load_first_w(3)
            load_x(3)
            sp.dma_start(ident[:], ident_d).then_inc(const_in, 16)
            sp.dma_start(level_f32, level_d).then_inc(const_in, 16)
            sp.dma_start(start_f32, start_d).then_inc(const_in, 16)
            sp.dma_start(fgain_sb[:], fgain).then_inc(const_in, 16)
            sp.dma_start(hgain_sb[:], hgain).then_inc(const_in, 16)
            sp.dma_start(lb_all[:, 3, :], lbl).then_inc(const_in, 16)
            sp.dma_start(relrow, relb).then_inc(const_in, 16)
            for d in range(4, KB):
                load_x(d)
                if d in (5, 6, 10, 12):
                    load_first_w({5: 4, 6: 5, 10: 6, 12: 7}[d])
            with sp.Fori(2, TILES) as g:
                load_w(g)
            for half in range(2):
                cols = slice(half * HALF, half * HALF + HALF)
                for c in range(KB):
                    sp.wait_ge(out_ready, half * KB + c + 1)
                    sp.dma_start(outT[c][:, cols], arr(c)[:, cols]).then_inc(out_stored, 16)
            sp.wait_ge(out_stored, 2 * 16 * KB)
            sp.wait_ge(y_stored, 16 * UNITS)

        @block.gpsimd
        def _(pool):
            nc.gpsimd.memset(ones_f32, 1.0).then_inc(ones_ready, 1)
            nc.gpsimd.memset(eps_sb[:], EPS).then_inc(ones_ready, 1)
            pool.wait_ge(ones_ready, 2)
            nc.gpsimd.tensor_tensor(ones[:], ones_f32, ones_f32, ALU.mult).then_inc(ones_ready, 1)
            pool.wait_ge(ones_ready, 3)

            def split_w(g, first=False):
                for q in range(NG):
                    pool.wait_ge(w_in[q], 16 * g + 16)
                    if not first:
                        pool.wait_ge(w_used, g * NG + (q + 1 - NG))
                    nc.gpsimd.tensor_tensor(w_hi[q][:], w_raw[q % RAW][:],
                                            ones[:].bitcast(F32)[:, None, :].to_broadcast([P, GRAN, P]),
                                            ALU.mult).then_inc(w_hi_done, 1)
                    pool.wait_ge(w_hi_done, g * NG + q + 1)
                    nc.gpsimd.tensor_tensor(w_lo[q][:], w_raw[q % RAW][:], w_hi[q][:].bitcast(F32),
                                            ALU.subtract).then_inc(w_split, 1)

            split_w(0, first=True)
            with pool.Fori(1, TILES) as g:
                split_w(g)

        @block.tensor
        def _(pe):
            def nothing():
                pass

            def project(g, pair, free, stages):
                pe.wait_ge(tile_evicted, free)
                for q in range(NG):
                    pe.wait_ge(w_split, g * NG + q + 1)
                    for kk in range(GRAN):
                        k = q * GRAN + kk
                        for wt, mv in ((w_hi, mv_hi), (w_hi, mv_lo), (w_lo, mv_hi)):
                            for half in range(2):
                                cols = slice(half * HALF, half * HALF + HALF)
                                last = nc.tensor.matmul(
                                    prj[pair][:, cols], wt[q][:, kk, :], mv[:, k, cols],
                                    start=(k == 0 and wt is w_hi and mv is mv_hi),
                                    stop=(k == KB - 1 and wt is w_lo))
                    last.then_inc(w_used, 1)
                    stages[q]()

            def project_pair(g, pairs, hi, lo, after_granule=(), before_last=nothing):
                steps = [(t, k) for k in range(KB - GRAN) for t in range(2)]
                steps += [(t, k) for t in range(2) for k in range(KB - GRAN, KB)]
                for t, k in steps:
                    s, kk = 2 * (k // GRAN) + t, k % GRAN
                    if (t, k) == (1, KB - GRAN):
                        before_last()
                    if t == 0:
                        pe.wait_ge(hi, k + 1)
                    if kk == 0:
                        pe.wait_ge(w_split, g * NG + s + 1)
                    for wt, mv in ((w_hi, mv_hi), (w_lo, mv_hi), (w_hi, mv_lo)):
                        if t == 0 and mv is mv_lo:
                            pe.wait_ge(lo, k + 1)
                        for half in range(2):
                            cols = slice(half * HALF, half * HALF + HALF)
                            last = nc.tensor.matmul(
                                prj[pairs[t]][:, cols], wt[s % NG][:, kk, :], mv[:, k, cols],
                                start=(k == 0 and wt is w_hi and mv is mv_hi),
                                stop=(k == KB - 1 and mv is mv_lo))
                    if kk == GRAN - 1:
                        last.then_inc(w_used, 1)
                    if t == 1 and kk == GRAN - 1 and k // GRAN < len(after_granule):
                        after_granule[k // GRAN]()

            def project_last(g, pair, free, between):
                pe.wait_ge(tile_evicted, free)
                for half in range(2):
                    cols = slice(half * HALF, half * HALF + HALF)
                    for k in range(KB):
                        q, kk = k // GRAN, k % GRAN
                        if kk == 0 and half == 0:
                            pe.wait_ge(w_split, g * NG + q + 1)
                        if half == 1 and k == GRAN:
                            between()
                        for wt, mv in ((w_hi, mv_hi), (w_hi, mv_lo), (w_lo, mv_hi)):
                            last = nc.tensor.matmul(
                                prj[pair][:, cols], wt[q][:, kk, :], mv[:, k, cols],
                                start=(k == 0 and wt is w_hi and mv is mv_hi),
                                stop=(k == KB - 1 and wt is w_lo))
                    last.then_inc(half_done, 1)

            def fill(n, before):
                if not (isinstance(before, int) and before == 0):
                    pe.wait_ge(drained[n], before)

            def transposes(n, src, wait, value, before):
                pe.wait_ge(const_in, 112)
                pe.wait_ge(wait, value)
                fill(n, before)
                for c in range(BLK):
                    last = nc.tensor.transpose(mixb(n)[:, c, :], blocks(src)[:, c, :], ident[:])
                last.then_inc(filled[n], 1)

            def a_vtr(u):
                return transposes(0, VT, tile_evicted, 4 * u + 3, A_M0 * u + 4)

            def part_sums(out, use):
                pe.wait_ge(parts_split, use + 1)
                nc.tensor.matmul(out, ones[:], part_hi[:], start=True, stop=False)
                return nc.tensor.matmul(out, ones[:], part_lo[:], start=False, stop=True)

            def a_diag(u, half):
                def stage():
                    cols = slice(half * HALF, half * HALF + HALF)
                    if half == 0:
                        fill(1, A_M1 * u)
                    last = part_sums(mix[1][:, cols], A_PARTS * u + half)
                    last.then_inc(first_part_used if half == 0 else filled[1], 1)
                return stage

            def a_near(u):
                def stage():
                    fill(0, A_M0 * u + 3)
                    part_sums(mix[0][:, 0:HALF], A_PARTS * u + 2).then_inc(filled[0], 1)
                return stage

            def a_level(u, n):
                def stage():
                    m = n % 2
                    pe.wait_ge(lv_ready, 2 * (NM * u + n + 1))
                    fill(m, (A_M0 * u + n // 2) if m == 0 else (A_M1 * u + 1 + n // 2))
                    size = LEVELS[n]
                    for c in range(BLK):
                        if n < WIDE:
                            for early in range(0, P, 2 * size):
                                late = early + size
                                last = nc.tensor.matmul(
                                    mixb(m)[early:early + size, c, late:late + size],
                                    blocks(LV[n % 2])[:, c, early:early + size],
                                    blocks(LV[n % 2])[:, c, late:late + size], start=True, stop=True)
                        else:
                            last = nc.tensor.matmul(mixb(m)[:, c, :], blocks(LV[n % 2])[:, c, :],
                                                    blocks(LV[n % 2])[:, c, :], start=True, stop=True)
                    last.then_inc(filled[m], 1)
                return stage

            def a_kdtr(u):
                def stage():
                    transposes(1, T3, kd_ready, u + 1, A_M1 * u + 4)
                    a_vtr(u)
                return stage

            def a_state(u):
                def stage():
                    pe.wait_ge(drained[1], A_M1 * u + 5)
                    pe.wait_ge(drained[0], A_M0 * u + 5)
                    for c in range(BLK - 1):
                        last = nc.tensor.matmul(mixb(1)[:, c, :], blocks(KDT)[:, c, :],
                                                blocks(V)[:, c, :], start=True, stop=True)
                    last.then_inc(filled[1], 1)
                return stage

            def a_out(u):
                def stage():
                    pe.wait_ge(drained[1], A_M1 * u + 6)
                    pe.wait_ge(qe_ready, u + 1)
                    fill(0, A_M0 * u + 5)
                    for c in range(BLK):
                        last = nc.tensor.matmul(mixb(0)[:, c, :], blocks(V)[:, c, :],
                                                blocks(SC)[:, c, :], start=True, stop=(c == 0))
                        if c > 0:
                            last = nc.tensor.matmul(mixb(0)[:, c, :], blocks(ST)[:, c, :],
                                                    blocks(QE)[:, c, :], start=False, stop=True)
                    last.then_inc(filled[0], 1)
                return stage

            def sum_squares(n, use, half, before):
                def stage():
                    cols = slice(half * HALF, half * HALF + HALF)
                    if half == 0:
                        fill(n, before)
                    last = part_sums(mix[n][:, cols], use + half)
                    last.then_inc(first_part_used if half == 0 else filled[n], 1)
                return stage

            def a_ss(u, half):
                return sum_squares(1, A_PARTS * u + 3, half, A_M1 * u + 6)

            def b_scores(i, p):
                pe.wait_ge(tile_evicted, TB + 4 * i + 2)
                fill(0, M0_B + B_M0 * i + 1 + p)
                nk = min(p + 1, B_BAND)
                first = p + 1 - nk
                for lo in range(0, nk * P, HALF):
                    hi = min(nk * P, lo + HALF)
                    last = nc.tensor.matmul(mix[0][:, lo:hi], blocks(BQ)[:, p, :],
                                            arr(BK)[:, first * P + lo:first * P + hi],
                                            start=True, stop=True)
                last.then_inc(filled[0], 1)

            def b_ptr(i, p):
                pe.wait_ge(p_ready, BLK * i + p + 1)
                fill(1, M1_B + B_M1 * i + 2 * p)
                nk = min(p + 1, B_BAND)
                for j in range(nk):
                    last = nc.tensor.transpose(mixb(1)[:, j, :], blocks(BP[p % 2])[:, j, :], ident[:])
                last.then_inc(filled[1], 1)

            def b_pv(i, p):
                fill(1, M1_B + B_M1 * i + 2 * p + 1)
                nk = min(p + 1, B_BAND)
                for j in range(nk):
                    last = nc.tensor.matmul(mixb(1)[:, 5, :], blocks(V)[:, p + 1 - nk + j, :],
                                            blocks(BT[p % 2])[:, j, :], start=(j == 0),
                                            stop=(j == nk - 1))
                last.then_inc(filled[1], 1)

            def b_visit(i, n):
                def stage():
                    if n >= 2:
                        b_pv(i, n - 2)
                    if n < BLK:
                        b_scores(i, n)
                    if 1 <= n <= BLK:
                        b_ptr(i, n - 1)
                return stage

            def b_vtr(i):
                return lambda: transposes(0, VT, tile_evicted, TB + 4 * i + 3, M0_B + B_M0 * i)

            def c_ktr(i):
                return lambda: transposes(1, CQK, c_rot, i + 1, M1_C + C_M1 * i)

            def c_vtr(i):
                return lambda: transposes(0, VT, tile_evicted, TC + 3 * i + 2, M0_C + C_M0 * i)

            def c_scores(i):
                def stage():
                    pe.wait_ge(c_k, i + 1)
                    pe.wait_ge(c_rot, i + 1)
                    fill(1, M1_C + C_M1 * i + 1)
                    for c in range(BLK):
                        last = nc.tensor.matmul(mixb(1)[:, c, :], blocks(CK)[:, c, :],
                                                blocks(CQK)[:, c, :], start=True, stop=True)
                    last.then_inc(filled[1], 1)
                return stage

            def c_state(i):
                def stage():
                    pe.wait_ge(drained[1], M1_C + C_M1 * i + 1)
                    fill(0, M0_C + C_M0 * i + 1)
                    kt = arena[:, CKT, 0:BLK * C_DK].rearrange("p (c k) -> p c k", c=BLK)
                    for c in range(BLK - 1):
                        last = nc.tensor.matmul(mixb(0)[0:C_DK, c, :], kt[:, c, :],
                                                blocks(V)[:, c, :], start=True, stop=True)
                    last.then_inc(filled[0], 1)
                return stage

            def c_out(i):
                def stage():
                    pe.wait_ge(drained[0], M0_C + C_M0 * i + 2)
                    pe.wait_ge(c_qd, i + 1)
                    fill(1, M1_C + C_M1 * i + 2)
                    for c in range(BLK):
                        last = nc.tensor.matmul(mixb(1)[:, c, :], blocks(V)[:, c, :],
                                                blocks(CSC)[:, c, :], start=True, stop=(c == 0))
                        if c > 0:
                            last = nc.tensor.matmul(mixb(1)[:, c, :], blocks(CST)[:, c, :],
                                                    blocks(CQD)[:, c, :], start=False, stop=True)
                    last.then_inc(filled[1], 1)
                return stage

            def c_ss(i, half):
                return sum_squares(0, PARTS_C + 2 * i, half, M0_C + C_M0 * i + 2)

            def a_late(u):
                return [a_level(u, 5), a_near(u), a_kdtr(u), a_state(u),
                        a_out(u), nothing, a_ss(u, 0), a_ss(u, 1)]

            def b_late(i):
                return [b_visit(i, 3), b_visit(i, 4), b_visit(i, 5), b_visit(i, 6),
                        b_visit(i, 7), b_visit(i, 8), b_visit(i, 9), nothing]

            def c_late(i):
                return [c_out(i), c_ss(i, 0), c_ss(i, 1), nothing, nothing, nothing, nothing, nothing]

            none8 = [nothing] * 8

            def ones_product(cols):
                return nc.tensor.matmul(mix[0][:, cols], ones[:].bitcast(F32), rstd[:, cols], start=True,
                                        stop=True)

            def start_tiles():
                def input_ss():
                    pe.wait_ge(ones_ready, 3)
                    pe.wait_ge(sq_added, KB)
                    for half in range(2):
                        last = ones_product(slice(half * HALF, half * HALF + HALF))
                    last.then_inc(ss_ready, 1)
                project_pair(0, (0, 1), h_hi, h_lo, before_last=input_ss)
                pe.wait_ge(rms_log, 1)

            def a_diag_level(u, both):
                def stage():
                    if both:
                        a_diag(u, 0)()
                    a_diag(u, 1)()
                    a_level(u, 0)()
                return stage

            def a_unit(u, late, start=False):
                g = 4 * u
                if start:
                    start_tiles()
                else:
                    project(g, 0, g - 1, late[0:4])
                    project(g + 1, 1, g, late[4:8])
                project(g + 2, 0, g + 1, [nothing, nothing, nothing if start else a_diag(u, 0),
                                        a_diag_level(u, both=start)])
                project(g + 3, 1, g + 2, [a_level(u, 1), a_level(u, 2), a_level(u, 3), a_level(u, 4)])

            def b_unit(i, late):
                g = TB + 4 * i
                project(g, 0, g - 1, late[0:4])
                project(g + 1, 1, g, late[4:8])
                project(g + 2, 0, g + 1, none8[0:4])
                project(g + 3, 1, g + 2, [b_vtr(i), b_visit(i, 0), b_visit(i, 1), b_visit(i, 2)])

            def c_unit(i, late, pair):
                g = TC + 3 * i
                project(g, pair, g - 1, late[0:4])
                project(g + 1, 1 - pair, g, none8[0:4])
                project(g + 2, pair, g + 1, [c_vtr_k(i), c_scores(i), c_state(i), nothing])

            def c_vtr_k(i):
                def stage():
                    c_ktr(i)()
                    c_vtr(i)()
                return stage

            a_unit(0, none8, start=True)
            with pe.Fori(1, A_HEADS) as u:
                a_unit(u, a_late(u - 1))
            b_unit(0, a_late(A_HEADS - 1))
            with pe.Fori(1, B_HEADS) as i:
                b_unit(i, b_late(i - 1))
            project(TC, 0, TC - 1, b_late(B_HEADS - 1)[0:4])
            project(TC + 1, 1, TC, b_late(B_HEADS - 1)[4:8])
            project(TC + 2, 0, TC + 1, [nothing, c_vtr_k(0), c_scores(0), c_state(0)])
            with pe.Fori(0, C_HEADS // 2) as j:
                c_unit(2 * j + 1, c_late(2 * j), 1)
                c_unit(2 * j + 2, c_late(2 * j + 1), 0)
            c_out(C_HEADS - 1)()

            pe.wait_ge(tile_evicted, TO)
            project_pair(TO, (1, 0), yl_hi, yl_lo, after_granule=[c_ss(C_HEADS - 1, 0), c_ss(C_HEADS - 1, 1)])
            with pe.Fori(1, KB // 2 - 1) as j:
                project(TO + 2 * j, 1, TO + 2 * j - 1, none8[0:4])
                project(TO + 2 * j + 1, 0, TO + 2 * j, none8[0:4])
            project(TILES - 2, 1, TILES - 3, none8[0:4])

            def output_ss(half):
                pe.wait_ge(sq_added, 2 * KB + half)
                ones_product(slice(half * HALF, half * HALF + HALF)).then_inc(ss_ready, 1)

            def first_output_ss():
                fill(0, M0_O)
                output_ss(0)

            project_last(TILES - 1, 0, TILES - 2, first_output_ss)
            output_ss(1)

        @block.scalar
        def _(act):
            def nothing():
                pass

            def exp(out, src, **kw):
                return nc.scalar.activation(out, src, ACT.Exp, **kw)

            def ln(out, src, **kw):
                return nc.scalar.activation(out, src, ACT.Ln, **kw)

            def inv_rms(src, dst, count, log_done):
                act.wait_ge(ones_ready, 2)
                ln(dst, src, scale=1.0 / count, bias=eps_sb[:, 0:1]).then_inc(*log_done[0:2])
                act.wait_ge(log_done[0], log_done[2])
                return exp(dst, dst, scale=-0.5)

            def sigmoid(m):
                act.wait_ge(silu_clamped, m + 1)
                exp(arr(T2), arr(T2), scale=-1.0).then_inc(silu_exp, 1)
                act.wait_ge(silu_exp, m + 1)
                ln(arr(T2), arr(T2), bias=1.0).then_inc(silu_log, 1)
                act.wait_ge(silu_log, m + 1)
                exp(arr(T2), arr(T2), scale=-1.0).then_inc(silu_sig, 1)

            def copy_v(fills):
                act.wait_ge(filled[0], fills)
                nc.scalar.activation(arr(V), mix[0][:], ACT.Copy).then_inc(drained[0], 1)

            def part_high(src):
                nc.scalar.activation(part_hi[:], src, ACT.Copy).then_inc(parts_hi, 1)

            def store_y(u):
                act.wait_ge(y_ready, u + 1)
                act.dma_start(y_dram[u], arr(Y)).then_inc(y_stored, 16)

            nc.scalar.preload_act_table_set("natural_log_exp_and_others")
            act.wait_ge(gain_in, 16)
            for d in range(KB):
                act.wait_ge(x_in[d % 4], 16 * (d // 4 + 1))
                nc.scalar.activation(mv_hi[:, d, :], arr(XS[d % 4]), ACT.Copy,
                                     scale=gain_sb[:, d:d + 1]).then_inc(h_hi, 1)
                if d >= 2:
                    act.wait_ge(sq_added, d - 1)
                nc.scalar.activation(arr(SQ[d % 2]), arr(XS[d % 4]), ACT.Square).then_inc(sq_ready, 1)
            act.wait_ge(start_dve, 1)
            exp(lb_all[:, 0, :], lb_all[:, 0, :]).then_inc(lb_exp, 1)
            act.wait_ge(rel_wide, 2)
            act.dma_start(rel_dram, arena[0:B_HEADS, Y, 0:BAND + P]).then_inc(y_stored, 16)
            act.wait_ge(ss_ready, 1)
            inv_rms(mix[0][:], rstd[:], D_MODEL, (rms_log, 1, 1)).then_inc(rstd_ready, 1)

            def a_decay(u):
                act.wait_ge(z_clamped, u + 1)
                exp(arr(LV1), arr(LV1), scale=-1.0).then_inc(z_exp, 1)
                act.wait_ge(z_exp, u + 1)
                ln(arr(T3), arr(LV1), bias=1.0).then_inc(z_log, 1)
                act.wait_ge(lb_copied, u + 1)
                ln(arr(B), arr(LV1), scale=lb_now[:, 0, :], bias=1.0).then_inc(z_loglb, 1)
                act.wait_ge(z_under, u + 1)
                act.wait_ge(z_log, u + 1)
                exp(arr(K), arr(T3), scale=-1.0).then_inc(z_sig, 1)

            def a_mix(u):
                sigmoid(2 * u)
                act.wait_ge(b_ready, 2 * u + 2)
                exp(arr(QE), arr(B)).then_inc(qe_exp, 1)
                exp(end_dec[:, :], blocks(B)[:, :, P - 1]).then_inc(end_ready, 1)
                act.wait_ge(kd_diff, u + 1)
                exp(arr(T3), arr(T3)).then_inc(kd_exp, 1)
                act.wait_ge(diag_prod, u + 1)
                part_high(arr(SC)[:, 0:HALF])
                for n in range(NM):
                    if n == 2:
                        act.wait_ge(first_part_used, 2 * u + 1)
                        part_high(arr(SC)[:, HALF:SEQ])
                    act.wait_ge(lv_diff, 2 * (NM * u + n + 1))
                    exp(arr(LV[n % 2]), arr(LV[n % 2])).then_inc(lv_exp, 1)
                sigmoid(2 * u + 1)
                act.wait_ge(near_diff, u + 1)
                exp(arr(LV0)[:, 0:HALF], arr(LV0)[:, 0:HALF]).then_inc(near_exp, 1)
                act.wait_ge(near_prod, 2 * u + 2)
                act.wait_ge(filled[1], A_M1 * u + 1)
                part_high(arr(LV0)[:, 0:HALF])
                act.wait_ge(filled[1], A_M1 * u + 5)
                nc.scalar.activation(arr(KDT), mix[1][:], ACT.Copy).then_inc(drained[1], 1)
                copy_v(A_M0 * u + 5)

            def a_finish(u):
                norm(u, 2 * u + 2, 0, A_M0 * u + 6, 1, A_M1 * u + 7, 2 * u + 2)
                store_y(u)

            def norm(m, gate, n_o, o_fills, n_ss, ss_fills, first_used, middle=nothing,
                     between=nothing):
                act.wait_ge(silu_done, gate)
                act.wait_ge(filled[n_o], o_fills)
                nc.scalar.activation(arr(T2), mix[n_o][:], ACT.Square).then_inc(osq_ready, 1)
                act.wait_ge(osq_ready, m + 1)
                part_high(arr(T2)[:, 0:HALF])
                middle()
                act.wait_ge(first_part_used, first_used)
                part_high(arr(T2)[:, HALF:SEQ])
                between()
                act.wait_ge(filled[n_ss], ss_fills)
                inv_rms(mix[n_ss][:], arr(T1), P, (drained[n_ss], 1, ss_fills)).then_inc(orms_ready, 1)

            a_decay(0)
            a_mix(0)
            with act.Fori(1, A_HEADS) as u:
                a_decay(u)
                a_finish(u - 1)
                a_mix(u)
            a_finish(A_HEADS - 1)

            def b_unit(i):
                act.wait_ge(drained[0], M0_B + B_M0 * i)
                act.dma_start(bias, bass.AP(tensor=rel_dram.tensor, offset=i * (BAND + P),
                                            ap=[[1, P], [1, BAND]])).then_inc(bias_in, 16)
                copy_v(M0_B + B_M0 * i + 1)
                for n in range(BLK + 2):
                    if n == 5:
                        sigmoid(2 * A_HEADS + i)
                    if n < BLK:
                        width = min(n + 1, B_BAND) * P
                        act.wait_ge(p_max, BLK * i + n + 1)
                        exp(arr(BP[n % 2])[:, 0:width], arr(BP[n % 2])[:, 0:width],
                            bias=row_max[:, n % 2, :], accum_out=row_sum[:, n % 2, :]).then_inc(p_exp, 1)
                    if 1 <= n <= BLK:
                        width = min(n, B_BAND) * P
                        act.wait_ge(filled[1], M1_B + B_M1 * i + 2 * n - 1)
                        nc.scalar.activation(arr(BT[(n - 1) % 2])[:, 0:width], mix[1][:, 0:width],
                                             ACT.Copy).then_inc(drained[1], 1)

            with act.Fori(0, B_HEADS - 1) as i:
                b_unit(i)
                store_y(B0 + i)
            b_unit(B_HEADS - 1)
            act.wait_ge(p_ready, BLK * B_HEADS)
            act.dma_start(arr(CCOS), rot_d[0]).then_inc(ctab_in, 16)
            act.dma_start(arr(CSIN), rot_d[1]).then_inc(ctab_in, 16)
            store_y(C0 - 1)

            def c_unit(i, first_y=nothing, early_y=nothing, middle_y=nothing, late_y=nothing):
                act.wait_ge(y_ready, C0 + i)
                act.dma_start(dec, dec_d[i]).then_inc(cdec_in, 16)
                act.wait_ge(tile_evicted, TC + 3 * i + 1)
                for t1 in (0, C_DK):
                    t2, end = t1 + C_DK // 2, t1 + C_DK
                    nc.scalar.activation(arena[t1:t2, T1, :], arena[t2:end, CQK, :], ACT.Copy,
                                         scale=-1.0).then_inc(c_partner, 1)
                    nc.scalar.activation(arena[t2:end, T1, :], arena[t1:t2, CQK, :],
                                         ACT.Copy).then_inc(c_partner, 1)
                act.wait_ge(c_rot, i + 1)
                act.wait_ge(c_zeroed, 2)
                nc.scalar.activation(arena[0:C_DK, CK, :], arena[C_DK:P, CQK, :], ACT.Copy,
                                     scale=C_DK ** -0.5).then_inc(c_k, 1)
                first_y()
                copy_v(M0_C + C_M0 * i + 1)
                early_y()
                sigmoid(2 * A_HEADS + B_HEADS + i)
                norm(A_HEADS + i, 2 * A_HEADS + B_HEADS + i + 1, 1, M1_C + C_M1 * i + 3, 0,
                     M0_C + C_M0 * i + 3, 2 * A_HEADS + i + 1, middle_y, late_y)

            def load_y(d):
                if d >= 4:
                    act.wait_ge(yl_lo, d - 3)
                act.dma_start(arr(YS[d % 4]), y_dram[d]).then_inc(yl_in[d % 4], 16)

            def y_hi(d, src):
                act.wait_ge(w_used, NG * (TO - 1) + d // GRAN + 1)
                nc.scalar.activation(mv_hi[:, d, :], src, ACT.Copy).then_inc(yl_hi, 1)

            def y_hi_loaded(d):
                act.wait_ge(yl_in[d % 4], 16 * (d // 4 + 1))
                y_hi(d, arr(YS[d % 4]))

            def first_y():
                act.wait_ge(y_stored, 16 * UNITS)
                for d in range(3):
                    load_y(d)

            def early_y():
                load_y(3)
                for d in range(8):
                    y_hi_loaded(d)
                    if d % 4 == 3:
                        for later in range(d + 1, d + 5):
                            load_y(later)

            def middle_y():
                for d in range(8, 12):
                    y_hi_loaded(d)

            def late_y():
                for d in range(12, KB - 1):
                    load_y(d)
                for d in range(12, KB - 1):
                    y_hi_loaded(d)

            act.wait_ge(y_ready, C0)
            for zeroed in (CK, CST):
                nc.scalar.activation(arena[C_DK:P, zeroed, :].rearrange("p (c t) -> p c t", c=BLK),
                                     ident[C_DK:P, None, :].to_broadcast([P - C_DK, BLK, P]), ACT.Copy,
                                     scale=0.0).then_inc(c_zeroed, 1)
            with act.Fori(0, C_HEADS - 1) as i:
                c_unit(i)
                store_y(C0 + i)
            c_unit(C_HEADS - 1, first_y, early_y, middle_y, late_y)
            act.wait_ge(y_ready, UNITS)
            y_hi(KB - 1, arr(Y))

            act.wait_ge(yl_lo, KB)
            for c in range(KB):
                act.dma_start(arr(c), xT[c]).then_inc(xr_in[c // 4], 16)

            with act.Fori(0, KB - 1) as c:
                act.wait_ge(tile_evicted, TO + c + 1)
                act.wait_ge(sq_added, KB + c)
                nc.scalar.activation(rstd[:], arr(c), ACT.Square).then_inc(sq_ready, 1)
            act.wait_ge(sq_added, 2 * KB - 1)
            for half in range(2):
                cols = slice(half * HALF, half * HALF + HALF)
                act.wait_ge(tile_evicted, TILES + half)
                nc.scalar.activation(rstd[:, cols], arr(KB - 1)[:, cols], ACT.Square).then_inc(sq_ready, 1)
                act.wait_ge(ss_ready, 2 + half)
                inv_rms(mix[0][:, cols], rstd[:, cols], D_MODEL,
                        (fin_log, 1, half + 1)).then_inc(fin_rstd, 1)

        @block.vector
        def _(dve):
            def nothing():
                pass

            tt = nc.vector.tensor_tensor
            ts = nc.vector.tensor_scalar
            stt = nc.vector.scalar_tensor_tensor

            def evict(g, pair, dst):
                dve.wait_ge(w_used, NG * g + NG)
                return tt(arr(dst), prj[pair][:], rstd[:], ALU.mult)

            def silu_evict(g, pair, m):
                evict(g, pair, T1).then_inc(tile_evicted, 1)
                dve.wait_ge(tile_evicted, g + 1)
                ts(arr(T2), arr(T1), -SAFE, None, ALU.max).then_inc(silu_clamped, 1)

            def silu_finish(m, dst, scale):
                dve.wait_ge(silu_sig, m + 1)
                stt(out=arr(dst), in0=arr(T1), scalar=scale, in1=arr(T2), op0=ALU.mult,
                    op1=ALU.mult).then_inc(silu_done, 1)

            def states(m, n, rows, st, fills, decay):
                dve.wait_ge(filled[n], fills)
                for c in range(BLK - 1):
                    cur = blocks(st)[0:rows, c + 1, :]
                    inc = mixb(n)[0:rows, c, :]
                    if c == 0:
                        new = nc.vector.tensor_copy(cur, inc)
                    else:
                        dve.wait_ge(state_ready, (BLK - 2) * m + c)
                        new = stt(out=cur, in0=blocks(st)[0:rows, c, :], scalar=decay(c), in1=inc,
                                  op0=ALU.mult, op1=ALU.add)
                    if c < BLK - 2:
                        new.then_inc(state_ready, 1)
                    else:
                        new.then_inc(drained[n], 1)

            dve.wait_ge(gain_in, 16)
            for d in range(KB):
                dve.wait_ge(x_in[d % 4], 16 * (d // 4 + 1))
                dve.wait_ge(h_hi, d + 1)
                stt(out=mv_lo[:, d, :], in0=arr(XS[d % 4]), scalar=gain_sb[:, d:d + 1],
                    in1=mv_hi[:, d, :].bitcast(F32), op0=ALU.mult, op1=ALU.subtract).then_inc(h_lo, 1)
                dve.wait_ge(sq_ready, d + 1)
                if d == 0:
                    nc.vector.tensor_copy(rstd[:], arr(SQ[0])).then_inc(sq_added, 1)
                else:
                    dve.wait_ge(sq_added, d)
                    tt(rstd[:], rstd[:], arr(SQ[d % 2]), ALU.add).then_inc(sq_added, 1)
            dve.wait_ge(const_in, 112)
            nc.vector.tensor_copy(level[:], level_f32).then_inc(masks_ready, 1)
            nc.vector.tensor_copy(scan_mask[:], start_f32).then_inc(masks_ready, 1)
            dve.wait_ge(masks_ready, 2)
            tt(lb_all[:, 0, :], lb_all[:, 3, :], lb_all[:, 3, :], ALU.subtract).then_inc(start_dve, 1)
            nc.vector.tensor_copy(arena[0:B_HEADS, Y, 0:REL - 2], relrow[:, 1:REL - 1]).then_inc(rel_wide, 1)
            nc.vector.tensor_copy(arena[0:B_HEADS, Y, REL - 2:BAND + P],
                                  relrow[:, REL - 1:REL].to_broadcast([B_HEADS, BAND + P - REL + 2])
                                  ).then_inc(rel_wide, 1)
            dve.wait_ge(lb_exp, 1)
            nc.vector.reciprocal(lb_all[:, 1, :], lb_all[:, 0, :]).then_inc(start_dve, 1)
            dve.wait_ge(start_dve, 2)
            tt(lb_all[:, 2, :], lb_all[:, 0, :], lb_all[:, 1, :], ALU.mult).then_inc(start_dve, 1)
            dve.wait_ge(start_dve, 3)
            tt(lb_all[:, 0, :], lb_all[:, 2, :], lb_all[:, 2, :], ALU.subtract).then_inc(start_dve, 1)
            dve.wait_ge(start_dve, 4)
            ts(lb_all[:, 1, :], lb_all[:, 0, :], -1.0, 1.0, ALU.mult, ALU.add).then_inc(start_dve, 1)
            ts(lb_all[:, 2, :], lb_all[:, 0, :], 0.0, None, ALU.is_equal).then_inc(start_dve, 1)
            dve.wait_ge(start_dve, 6)
            dve.wait_ge(y_stored, 16)
            dve.wait_ge(rstd_ready, 1)
            dve.wait_ge(w_used, 2 * NG - 1)

            def lv_view(n, size):
                return arr(n).rearrange("p (a h t) -> p a h t", h=2, t=size)

            def lv_diff_of(u, n):
                size = LEVELS[n]
                if n >= 2:
                    m = n % 2
                    dve.wait_ge(filled[m], (A_M0 * u + n // 2) if m == 0 else (A_M1 * u + 1 + n // 2))
                b, lv = lv_view(B, size), lv_view(LV[n % 2], size)
                ref = b[:, :, 0, size - 1:size].to_broadcast([P, SEQ // (2 * size), size])
                tt(lv[:, :, 1, :], b[:, :, 1, :], ref, ALU.subtract).then_inc(lv_diff, 1)
                tt(lv[:, :, 0, :], ref, b[:, :, 0, :], ALU.subtract).then_inc(lv_diff, 1)

            def lv_mult(u, n):
                size = LEVELS[n]
                lv = lv_view(LV[n % 2], size)
                dve.wait_ge(lv_exp, NM * u + n + 1)
                tt(lv[:, :, 1, :], lv[:, :, 1, :], lv_view(Q, size)[:, :, 1, :],
                   ALU.mult).then_inc(lv_ready, 1)
                tt(lv[:, :, 0, :], lv[:, :, 0, :], lv_view(K, size)[:, :, 0, :],
                   ALU.mult).then_inc(lv_ready, 1)

            def near_diff_of(u):
                dve.wait_ge(filled[0], A_M0 * u + 3)
                b = lv_view(B, 1)
                tt(arr(LV0)[:, 0:HALF], b[:, :, 1, 0], b[:, :, 0, 0], ALU.subtract).then_inc(near_diff, 1)

            def near_mult(u):
                dve.wait_ge(near_exp, u + 1)
                near = arr(LV0)[:, 0:HALF]
                tt(near, near, lv_view(Q, 1)[:, :, 1, 0], ALU.mult).then_inc(near_prod, 1)
                dve.wait_ge(near_prod, 2 * u + 1)
                tt(near, near, lv_view(K, 1)[:, :, 0, 0], ALU.mult).then_inc(near_prod, 1)

            def part_low(src, use):
                dve.wait_ge(parts_hi, use + 1)
                tt(part_lo[:], src, part_hi[:].bitcast(F32), ALU.subtract).then_inc(parts_split, 1)

            def near_drain(u):
                dve.wait_ge(filled[0], A_M0 * u + 4)
                dve.wait_ge(drained[1], A_M1 * u + 4)
                nc.vector.memset(wait_pad[:], 0.0)
                odd = blocks(SC).rearrange("p c (t two) -> p c t two", two=2)[:, :, :, 1]
                mask = level[:, NM - WIDE:NM - WIDE + 1, 1::2].to_broadcast([P, BLK, P // 2])
                nc.vector.copy_predicated(odd, mask, mix[0][:, 0:HALF].rearrange(
                    "p (c t) -> p c t", c=BLK)).then_inc(drained[0], 1)

            def lv_drain(u, n):
                m, size = n % 2, LEVELS[n]
                dve.wait_ge(filled[m], (A_M0 * u + 1 + n // 2) if m == 0 else (A_M1 * u + 2 + n // 2))
                dve.wait_ge(drained[1 - m], (A_M1 * u + 1 + n // 2) if m == 0 else (A_M0 * u + 1 + n // 2))
                if n < WIDE:
                    for early in range(0, P, 2 * size):
                        late = early + size
                        last = nc.vector.tensor_copy(blocks(SC)[early:early + size, :, late:late + size],
                                                     mixb(m)[early:early + size, :, late:late + size])
                    last.then_inc(drained[m], 1)
                    return
                nc.vector.memset(wait_pad[:], 0.0)
                mask = level[:, n - WIDE:n - WIDE + 1, :].to_broadcast([P, BLK, P])
                nc.vector.copy_predicated(blocks(SC), mask, mixb(m)).then_inc(drained[m], 1)

            def a_decay(u):
                g = 4 * u
                nc.vector.tensor_copy(lb_now[:], lb_all[:, :, bass.ds(u, 1)]).then_inc(lb_copied, 1)
                evict(g, 0, K).then_inc(tile_evicted, 1)
                dve.wait_ge(tile_evicted, g + 1)
                ts(arr(LV1), arr(K), -SAFE, None, ALU.max).then_inc(z_clamped, 1)
                dve.wait_ge(z_clamped, u + 1)
                ts(arr(LV0), arr(K), SAFE, 0.0, ALU.add, ALU.min).then_inc(z_under, 1)
                dve.wait_ge(z_loglb, u + 1)
                dve.wait_ge(z_under, u + 1)
                dve.wait_ge(lb_copied, u + 1)
                stt(out=arr(LV0), in0=arr(LV0), scalar=lb_now[:, 2, :], in1=arr(B), op0=ALU.mult,
                    op1=ALU.add).then_inc(z_sum, 1)
                dve.wait_ge(z_log, u + 1)
                dve.wait_ge(z_sum, u + 1)
                tt(arr(LV0), arr(LV0), arr(T3), ALU.subtract).then_inc(logf_ready, 1)
                dve.wait_ge(z_sig, u + 1)
                stt(out=arr(K), in0=arr(LV1), scalar=lb_now[:, 1, :], in1=arr(K), op0=ALU.mult,
                    op1=ALU.mult).then_inc(k_ready, 1)
                dve.wait_ge(logf_ready, u + 1)
                for half in range(2):
                    cols = slice(half * HALF, half * HALF + HALF)
                    nc.vector.tensor_tensor_scan(arr(B)[:, cols], scan_mask[:], arr(LV0)[:, cols], 0.0,
                                                 ALU.mult, ALU.add).then_inc(b_ready, 1)
                dve.wait_ge(b_ready, 2 * u + 2)
                dve.wait_ge(k_ready, u + 1)
                ends = blocks(B)[:, :, P - 1:P].to_broadcast([P, BLK, P])
                tt(blocks(T3), ends, blocks(B), ALU.subtract).then_inc(kd_diff, 1)

            def a_mix(u):
                g = 4 * u
                silu_evict(g + 1, 1, 2 * u)
                lv_diff_of(u, 0)
                lv_diff_of(u, 1)
                silu_finish(2 * u, Q, A_DK ** -0.5)
                dve.wait_ge(silu_done, 2 * u + 1)
                tt(arr(SC), arr(Q), arr(K), ALU.mult).then_inc(diag_prod, 1)
                dve.wait_ge(qe_exp, u + 1)
                tt(arr(QE), arr(QE), arr(Q), ALU.mult).then_inc(qe_ready, 1)
                dve.wait_ge(kd_exp, u + 1)
                tt(arr(T3), arr(T3), arr(K), ALU.mult).then_inc(kd_ready, 1)
                part_low(arr(SC)[:, 0:HALF], A_PARTS * u)
                lv_mult(u, 0)
                lv_mult(u, 1)
                part_low(arr(SC)[:, HALF:SEQ], A_PARTS * u + 1)
                dve.wait_ge(filled[1], A_M1 * u + 1)
                tt(blocks(SC), mixb(1), ident[:, None, :].to_broadcast([P, BLK, P]),
                   ALU.mult).then_inc(drained[1], 1)
                evict(g + 2, 0, VT).then_inc(tile_evicted, 1)
                for n in range(NM):
                    if n + 2 < NM:
                        lv_diff_of(u, n + 2)
                    if n == 4:
                        near_diff_of(u)
                    lv_drain(u, n)
                    if n == 3:
                        silu_evict(g + 3, 1, 2 * u + 1)
                    if n + 2 < NM:
                        lv_mult(u, n + 2)
                    if n == 4:
                        near_mult(u)
                        silu_finish(2 * u + 1, GATE, 1.0)
                        part_low(arr(LV0)[:, 0:HALF], A_PARTS * u + 2)
                near_drain(u)
                dve.wait_ge(end_ready, u + 1)
                states(u, 1, P, ST, A_M1 * u + 6, lambda c: end_dec[:, c:c + 1])

            def a_finish(u):
                finish_y(u, u, 2 * u + 2, 0, A_M0 * u + 6, hgain_sb[:, 0:1], A_PARTS * u + 3)

            def finish_y(u, m, gate, n, o_drain, scale, use, middle=nothing, between=nothing):
                part_low(arr(T2)[:, 0:HALF], use)
                middle()
                part_low(arr(T2)[:, HALF:SEQ], use + 1)
                between()
                dve.wait_ge(orms_ready, m + 1)
                dve.wait_ge(y_stored, 16 * u + 16)
                stt(out=arr(Y), in0=mix[n][:], scalar=scale, in1=arr(T1), op0=ALU.mult,
                    op1=ALU.mult).then_inc(drained[n], 1)
                dve.wait_ge(drained[n], o_drain)
                dve.wait_ge(silu_done, gate)
                tt(arr(Y), arr(Y), arr(GATE), ALU.mult).then_inc(y_ready, 1)

            a_decay(0)
            a_mix(0)
            with dve.Fori(1, A_HEADS) as u:
                a_decay(u)
                a_finish(u - 1)
                a_mix(u)

            def b_block(i, p):
                nk = min(p + 1, B_BAND)
                w, m = nk * P, p % 2
                dve.wait_ge(filled[0], M0_B + B_M0 * i + 2 + p)
                if p >= 2:
                    dve.wait_ge(filled[1], M1_B + B_M1 * i + 2 * p - 3)
                stt(out=arr(BP[m])[:, 0:w], in0=mix[0][:, 0:w], scalar=B_DH ** -0.5,
                    in1=bias[:, 0:w][:, ::-1], op0=ALU.mult, op1=ALU.add).then_inc(drained[0], 1)
                dve.wait_ge(drained[0], M0_B + B_M0 * i + 2 + p)
                nc.vector.tensor_reduce(row_max[:, m, :], arr(BP[m])[:, 0:w], AX_X, ALU.max,
                                        negate=True).then_inc(p_max, 1)
                dve.wait_ge(p_exp, BLK * i + p + 1)
                nc.vector.reciprocal(row_inv[:, m, :], row_sum[:, m, :]).then_inc(p_inv, 1)
                dve.wait_ge(p_inv, BLK * i + p + 1)
                ts(arr(BP[m])[:, 0:w], arr(BP[m])[:, 0:w], row_inv[:, m, :], None,
                   ALU.mult).then_inc(p_ready, 1)

            def b_out(i, p):
                dve.wait_ge(filled[1], M1_B + B_M1 * i + 2 * p + 2)
                nc.vector.tensor_copy(blocks(Y)[:, p, :], mixb(1)[:, 5, :]).then_inc(drained[1], 1)

            def b_unit(i, first=False):
                g = TB + 4 * i
                evict(g, 0, BQ).then_inc(tile_evicted, 1)
                if first:
                    a_finish(A_HEADS - 1)
                evict(g + 1, 1, BK).then_inc(tile_evicted, 1)
                dve.wait_ge(bias_in, 16 * i + 16)
                nc.vector.memset(bias[0:P // 2, 0:P // 2], NEG_INF).then_inc(bias_ready, 1)
                nc.vector.memset(bias[P // 2:P, BAND - P // 2:BAND], NEG_INF).then_inc(bias_ready, 1)
                evict(g + 2, 0, VT).then_inc(tile_evicted, 1)
                dve.wait_ge(bias_ready, 2 * i + 2)
                dve.wait_ge(y_stored, 16 * (B0 + i) + 16)
                for n in range(BLK + 2):
                    if n >= 2:
                        b_out(i, n - 2)
                    if n < BLK:
                        b_block(i, n)
                    if n == 4:
                        silu_evict(g + 3, 1, 2 * A_HEADS + i)
                silu_finish(2 * A_HEADS + i, GATE, 1.0)
                dve.wait_ge(silu_done, 2 * A_HEADS + i + 1)
                dve.wait_ge(drained[1], M1_B + B_M1 * (i + 1))
                tt(arr(Y), arr(Y), arr(GATE), ALU.mult).then_inc(y_ready, 1)

            b_unit(0, first=True)
            with dve.Fori(1, B_HEADS) as i:
                b_unit(i)

            def y_lo(d, src):
                dve.wait_ge(yl_hi, d + 1)
                tt(mv_lo[:, d, :], src, mv_hi[:, d, :].bitcast(F32), ALU.subtract).then_inc(yl_lo, 1)

            def y_lo_loaded(first, end):
                for d in range(first, end):
                    dve.wait_ge(yl_in[d % 4], 16 * (d // 4 + 1))
                    y_lo(d, arr(YS[d % 4]))

            def c_unit(i, pair, last=False):
                g = TC + 3 * i
                heads = A_HEADS + i
                evict(g, pair, CQK).then_inc(tile_evicted, 1)
                dve.wait_ge(tile_evicted, g + 1)
                tt(arr(T2), arr(CQK), arr(CCOS), ALU.mult).then_inc(c_cos, 1)
                dve.wait_ge(c_partner, 4 * i + 4)
                tt(arr(T3), arr(T1), arr(CSIN), ALU.mult).then_inc(c_sin, 1)
                dve.wait_ge(c_cos, i + 1)
                dve.wait_ge(c_sin, i + 1)
                tt(arr(CQK), arr(T2), arr(T3), ALU.add).then_inc(c_rot, 1)
                dve.wait_ge(c_rot, i + 1)
                dve.wait_ge(cdec_in, 16 * i + 16)
                tt(blocks(CQD), blocks(CQK), dec[:, None, P:2 * P].to_broadcast([P, BLK, P]),
                   ALU.mult).then_inc(c_qd, 1)
                evict(g + 1, 1 - pair, VT).then_inc(tile_evicted, 1)
                dve.wait_ge(filled[1], M1_C + C_M1 * i + 1)
                ts(arena[:, CKT, 0:BLK * C_DK].rearrange("p (c k) -> p c k", c=BLK),
                   mixb(1)[:, :, C_DK:P], dec[:, 2 * P:2 * P + 1], C_DK ** -0.5, ALU.mult,
                   ALU.mult).then_inc(drained[1], 1)
                dve.wait_ge(filled[1], M1_C + C_M1 * i + 2)
                tt(blocks(CSC), mixb(1), dec[:, None, 0:P].to_broadcast([P, BLK, P]),
                   ALU.mult).then_inc(drained[1], 1)
                if last:
                    y_lo_loaded(0, 4)
                states(heads, 0, C_DK, CST, M0_C + C_M0 * i + 2,
                       lambda c: dec[0:C_DK, 2 * P + 1:2 * P + 2])
                m = 2 * A_HEADS + B_HEADS + i
                if last:
                    y_lo_loaded(4, 8)
                silu_evict(g + 2, pair, m)
                silu_finish(m, GATE, 1.0)
                finish_y(C0 + i, heads, m + 1, 1, M1_C + C_M1 * i + 3, 1.0, PARTS_C + 2 * i,
                         (lambda: y_lo_loaded(8, 12)) if last else nothing,
                         (lambda: y_lo_loaded(12, KB - 1)) if last else nothing)

            dve.wait_ge(ctab_in, 32)
            with dve.Fori(0, C_HEADS // 2) as j:
                c_unit(2 * j, 0)
                c_unit(2 * j + 1, 1)
            c_unit(C_HEADS - 1, 0, last=True)
            dve.wait_ge(y_ready, UNITS)
            y_lo(KB - 1, arr(Y))

            def residual(c, pair, cols=slice(0, SEQ)):
                return tt(arr(c)[:, cols], prj[pair][:, cols], arr(c)[:, cols],
                          ALU.add).then_inc(tile_evicted, 1)

            def add_squares(c):
                dve.wait_ge(sq_ready, KB + c + 1)
                dve.wait_ge(sq_added, KB + c)
                tt(mix[1][:], mix[1][:], rstd[:], ALU.add).then_inc(sq_added, 1)

            def scale_half(half, first, end):
                cols = slice(half * HALF, half * HALF + HALF)
                dve.wait_ge(fin_rstd, half + 1)
                for c in range(first, end):
                    stt(out=arr(c)[:, cols], in0=arr(c)[:, cols], scalar=fgain_sb[:, c:c + 1],
                        in1=rstd[:, cols], op0=ALU.mult, op1=ALU.mult).then_inc(out_ready, 1)

            dve.wait_ge(w_used, NG * (TO + 2) - 1)
            dve.wait_ge(xr_in[0], 16 * 4)
            residual(0, 1)
            dve.wait_ge(w_used, NG * (TO + 2))
            residual(1, 0)
            dve.wait_ge(sq_ready, KB + 1)
            nc.vector.tensor_copy(mix[1][:], rstd[:]).then_inc(sq_added, 1)
            add_squares(1)
            for group in range(1, 4):
                dve.wait_ge(xr_in[group], 16 * 4)
            with dve.Fori(1, KB // 2 - 1) as j:
                for c, pair in ((2 * j, 1), (2 * j + 1, 0)):
                    dve.wait_ge(w_used, NG * (TO + c) + NG)
                    residual(c, pair)
                    add_squares(c)
            dve.wait_ge(w_used, NG * (TILES - 1))
            residual(KB - 2, 1)
            add_squares(KB - 2)
            def last_residual(half):
                cols = slice(half * HALF, half * HALF + HALF)
                dve.wait_ge(half_done, half + 1)
                residual(KB - 1, 0, cols)

            def last_squares(half):
                cols = slice(half * HALF, half * HALF + HALF)
                dve.wait_ge(sq_ready, 2 * KB + half)
                dve.wait_ge(sq_added, 2 * KB - 1)
                tt(rstd[:, cols], mix[1][:, cols], rstd[:, cols], ALU.add).then_inc(sq_added, 1)

            last_residual(0)
            last_squares(0)
            scale_half(0, 0, 9)
            last_residual(1)
            scale_half(0, 9, 10)
            last_squares(1)
            scale_half(0, 10, KB)
            scale_half(1, 0, KB)


def layouts(x, w_in, norm_gain, lb_logits, hgrn_norm_gain, rel_bias, w_out, final_gain):
    sizes = [A_HEADS * A_DK] * 4 + [B_HEADS * B_DH] * 4 + [C_HEADS * C_DK] * 2 + [C_HEADS * P] * 2
    at = np.concatenate([[0], np.cumsum(sizes)])
    aq, af, ai, ag, bq, bk, bv, bg, cq, ck, cv, cg = [int(n) for n in at[:-1]]
    cols = []
    for h in range(A_HEADS):
        cols += [np.arange(s + P * h, s + P * h + P) for s in (af, aq, ai, ag)]
    for h in range(B_HEADS):
        cols += [np.arange(s + P * h, s + P * h + P) for s in (bq, bk, bv, bg)]
    for h in range(C_HEADS):
        cols += [np.arange(s + C_DK * h, s + C_DK * h + C_DK) for s in (cq, ck)]
        cols += [np.arange(s + P * h, s + P * h + P) for s in (cv, cg)]
    cols = np.concatenate(cols)

    def tiles(m):
        return m.reshape(NG, GRAN, P, -1, P).transpose(3, 2, 0, 1, 4)

    w = np.concatenate([tiles(w_in[0][:, cols]), tiles(w_out[0])])
    for g in (0, TO):
        both = w[g:g + 2].transpose(2, 0, 1, 3, 4).reshape(2, NG, P, GRAN, P)
        w[g:g + 2] = both.transpose(0, 2, 1, 3, 4)
    return {"xT": np.ascontiguousarray(x[0].T).reshape(KB, P, SEQ), "w": np.ascontiguousarray(w),
            "gain": np.ascontiguousarray(norm_gain[0].reshape(KB, P).T),
            "lbl": np.ascontiguousarray(lb_logits[0].reshape(A_HEADS, P).T),
            "hgain": np.ascontiguousarray(hgrn_norm_gain[0].reshape(P, 1)),
            "relb": np.ascontiguousarray(rel_bias[0]),
            "fgain": np.ascontiguousarray(final_gain.reshape(KB, P).T)}


def kernel(**inputs):
    import concourse.bacc as bacc
    from concourse.bass_utils import run_bass_kernel_spmd

    arrays = layouts(**{name: np.asarray(a) for name, a in inputs.items()})
    arrays.update(shape_tables())
    nc = bacc.Bacc("TRN2", target_bir_lowering=False, num_devices=1, dynamic_dma_scratch_size=1024)
    args = [nc.dram_tensor(f"in_{name}", a.shape, mybir.dt.from_np(a.dtype), kind="ExternalInput").ap()
            for name, a in arrays.items()]
    out = nc.dram_tensor("outT", (KB, P, SEQ), F32, kind="ExternalOutput").ap()
    build(nc, *args, out)
    r = run_bass_kernel_spmd(nc, [{f"in_{name}": a for name, a in arrays.items()}], core_ids=[0])
    got = np.asarray(r.results[0]["outT"])
    return np.ascontiguousarray(got.reshape(D_MODEL, SEQ).T).reshape(1, SEQ, D_MODEL)
```
